# Optimizing a Trainium2 kernel written in Bass

```python
import math
import jax
import jax.numpy as jnp
from jax import lax
import numpy as np

D_MODEL = 1024
BATCH = 1
SEQ = 512
DEPTH = 1
DEC_BATCH = 8
DEC_SEQ = 1
PAST_LEN = 4096
PAGE_SIZE = 128

HEAD_DIM = 64
NSA_HEADS = 8
NSA_KV_HEADS = 2
NSA_GROUP = NSA_HEADS // NSA_KV_HEADS
NSA_WIDTH = NSA_HEADS * HEAD_DIM
CMP_BLOCK = 32
CMP_STRIDE = 16
CMP_UNITS = CMP_BLOCK // CMP_STRIDE
SEL_BLOCK = 64
N_SELECT = 16
WINDOW = 512
DIFF_HEADS = 8
DIFF_QK_DIM = 32
DIFF_V_DIM = 2 * DIFF_QK_DIM
DIFF_WIDTH = DIFF_HEADS * DIFF_V_DIM
MIX_WIDTH = NSA_WIDTH + DIFF_WIDTH
KV_COLS = 2 * NSA_KV_HEADS * HEAD_DIM
DIFF_QK_COLS = DIFF_HEADS * 2 * DIFF_QK_DIM
PROJ_COLS = NSA_WIDTH + 3 * KV_COLS + 3 * NSA_HEADS + NSA_WIDTH + 2 * DIFF_QK_COLS + 2 * DIFF_WIDTH
ROPE_THETA = 500000.0
ROT_FRACTION = 4
Q_BLOCK = 128
NSA_Q_BLOCK = 64
NORM_EPS = 1e-6
NEG_INF = -1e30
FORCE_SCORE = 1e9

kernel_name = 'hymba_nsa_diffattn_decode_step'

def rms_norm(x, w):
    xf = x.astype(jnp.float32)
    y = xf * lax.rsqrt(jnp.mean(xf * xf, axis=-1, keepdims=True) + NORM_EPS)
    return (y * w.astype(jnp.float32)).astype(x.dtype)

def rope(x, pos):
    rot = x.shape[-1] // ROT_FRACTION
    half = rot // 2
    inv = ROPE_THETA ** (-jnp.arange(half, dtype=jnp.float32) / half)
    ang = pos.astype(jnp.float32)[:, None] * inv
    ang = ang.reshape(ang.shape[:1] + (1,) * (x.ndim - 3) + (half,))
    cos, sin = jnp.cos(ang), jnp.sin(ang)
    xf = x[..., :rot].astype(jnp.float32)
    x1, x2 = xf[..., :half], xf[..., half:]
    rotated = jnp.concatenate([x1 * cos - x2 * sin, x2 * cos + x1 * sin], axis=-1).astype(x.dtype)
    return jnp.concatenate([rotated, x[..., rot:]], axis=-1)

def masked_softmax(s, mask):
    s = jnp.where(mask, s, NEG_INF)
    e = jnp.where(mask, jnp.exp(s - jnp.max(s, axis=-1, keepdims=True)), 0.0)
    return e / jnp.maximum(jnp.sum(e, axis=-1, keepdims=True), 1e-30)

def split_proj(proj):
    sizes = (NSA_WIDTH, KV_COLS, KV_COLS, KV_COLS, 3 * NSA_HEADS, NSA_WIDTH,
             DIFF_QK_COLS, DIFF_QK_COLS, DIFF_WIDTH, DIFF_WIDTH)
    return jnp.split(proj, [int(c) for c in np.cumsum(sizes)[:-1]], axis=-1)

def pad_to_multiple(rows, size):
    pad = (-rows.shape[1]) % size
    return jnp.pad(rows, ((0, 0), (0, pad)) + ((0, 0),) * (rows.ndim - 2))

def project(x, pos, lp):
    B, T, _ = x.shape
    h = rms_norm(x, lp['norm_w'])
    q_n, kv_c, kv_s, kv_w, g_n, z_n, q_d, k_d, v_d, z_d = split_proj(h @ lp['w_in'])
    q_n = rope(rms_norm(q_n.reshape(B, T, NSA_HEADS, HEAD_DIM), lp['nsa_q_norm']), pos)
    q_n = q_n.reshape(B, T, NSA_KV_HEADS, NSA_GROUP, HEAD_DIM) * HEAD_DIM ** -0.5
    kv_c = kv_c.reshape(B, T, 2, NSA_KV_HEADS, HEAD_DIM)
    kv_s = kv_s.reshape(B, T, 2, NSA_KV_HEADS, HEAD_DIM)
    kv_s = jnp.stack([rope(rms_norm(kv_s[:, :, 0], lp['nsa_ks_norm']), pos), kv_s[:, :, 1]], axis=2)
    kv_w = kv_w.reshape(B, T, 2, NSA_KV_HEADS, HEAD_DIM)
    kv_w = jnp.stack([rope(rms_norm(kv_w[:, :, 0], lp['nsa_kw_norm']), pos), kv_w[:, :, 1]], axis=2)
    g_n = jax.nn.sigmoid(g_n.astype(jnp.float32)).reshape(B, T, 3, NSA_KV_HEADS, NSA_GROUP).astype(x.dtype)
    q_d = rope(rms_norm(q_d.reshape(B, T, DIFF_HEADS, 2, DIFF_QK_DIM), lp['diff_q_norm']), pos) * DIFF_QK_DIM ** -0.5
    k_d = rope(rms_norm(k_d.reshape(B, T, DIFF_HEADS, 2, DIFF_QK_DIM), lp['diff_k_norm']), pos)
    v_d = v_d.reshape(B, T, DIFF_HEADS, DIFF_V_DIM)
    return q_n, kv_c, kv_s, kv_w, g_n, z_n, q_d, k_d, v_d, z_d

def compress(rows, pos_emb, w1, w2):
    B, L, G, D = rows.shape
    n_units = L // CMP_STRIDE
    n_cmp = n_units - CMP_UNITS + 1
    units = rows[:, :n_units * CMP_STRIDE].reshape(B, n_units, CMP_STRIDE, G, D)
    blocks = jnp.concatenate([units[:, j:j + n_cmp] for j in range(CMP_UNITS)], axis=2)
    hid = jax.nn.silu(jnp.einsum('bnlgd,lde->bnge', blocks + pos_emb[:, None, :], w1))
    return jnp.einsum('bnge,ef->bngf', hid, w2)

def compressed_kv(kv_c, lp):
    kc = compress(kv_c[:, :, 0], lp['cmp_pos_k'], lp['cmp_w1_k'], lp['cmp_w2_k'])
    vc = compress(kv_c[:, :, 1], lp['cmp_pos_v'], lp['cmp_w1_v'], lp['cmp_w2_v'])
    cend = jnp.arange(kc.shape[1]) * CMP_STRIDE + CMP_BLOCK - 1
    kc = rope(rms_norm(kc, lp['nsa_kc_norm']), cend)
    return kc, vc, cend

def selection_overlap(n_cmp, n_sel):
    cs = np.arange(n_cmp)[:, None] * CMP_STRIDE
    ss = np.arange(n_sel)[None, :] * SEL_BLOCK
    ov = np.minimum(cs + CMP_BLOCK, ss + SEL_BLOCK) - np.maximum(cs, ss)
    return jnp.asarray(np.clip(ov, 0, None) / CMP_STRIDE, dtype=jnp.float32)

def nsa_cmp_sel(q, qpos, kc, vc, cend, k_sel, v_sel, overlap):
    B, Tq, G = q.shape[:3]
    D = q.shape[-1]
    s = jnp.einsum('btgrd,bngd->btgrn', q, kc).astype(jnp.float32)
    p_cmp = masked_softmax(s, (cend[None, :] <= qpos[:, None])[None, :, None, None, :])
    o_cmp = jnp.einsum('btgrn,bngd->btgrd', p_cmp.astype(vc.dtype), vc)
    n_sel = overlap.shape[1]
    imp = jnp.einsum('btgrn,nj->btgj', p_cmp, overlap)
    blk = jnp.arange(n_sel)[None, :]
    cur = (qpos // SEL_BLOCK)[:, None]
    valid = blk * SEL_BLOCK <= qpos[:, None]
    forced = (blk == 0) | (blk == cur) | (blk == cur - 1)
    imp = jnp.where(forced[None, :, None, :], FORCE_SCORE, jnp.where(valid[None, :, None, :], imp, NEG_INF))
    _, idx = lax.top_k(imp, min(N_SELECT, n_sel))
    kb = k_sel.reshape(B, n_sel, SEL_BLOCK, G, D).transpose(0, 3, 1, 2, 4)
    vb = v_sel.reshape(B, n_sel, SEL_BLOCK, G, D).transpose(0, 3, 1, 2, 4)
    bi = jnp.arange(B)[:, None, None, None]
    gi = jnp.arange(G)[None, None, :, None]
    n_keys = idx.shape[-1] * SEL_BLOCK
    kg = kb[bi, gi, idx].reshape(B, Tq, G, n_keys, D)
    vg = vb[bi, gi, idx].reshape(B, Tq, G, n_keys, D)
    kpos = (idx[..., None] * SEL_BLOCK + jnp.arange(SEL_BLOCK)).reshape(B, Tq, G, n_keys)
    s2 = jnp.einsum('btgrd,btgsd->btgrs', q, kg).astype(jnp.float32)
    p_sel = masked_softmax(s2, (kpos <= qpos[None, :, None, None])[:, :, :, None, :])
    o_sel = jnp.einsum('btgrs,btgsd->btgrd', p_sel.astype(vg.dtype), vg)
    return o_cmp, o_sel

def window_attend(q, k, v, qpos, kpos):
    s = jnp.einsum('btgrd,bsgd->btgrs', q, k).astype(jnp.float32)
    d = qpos[:, None] - kpos[None, :]
    mask = (d >= 0) & (d < WINDOW) & (kpos[None, :] >= 0)
    p = masked_softmax(s, mask[None, :, None, None, :])
    return jnp.einsum('btgrs,bsgd->btgrd', p.astype(v.dtype), v)

def diff_attend(q, k, v, qpos, kpos, lam):
    s = jnp.einsum('bqhcd,bkhcd->bhcqk', q, k).astype(jnp.float32)
    p = masked_softmax(s, kpos[None, :] <= qpos[:, None])
    a = p[:, :, 0] - lam * p[:, :, 1]
    return jnp.einsum('bhqk,bkhv->bqhv', a.astype(v.dtype), v)

def diff_lambda(lp, lam_init):
    f32 = jnp.float32
    return (jnp.exp(jnp.sum(lp['lambda_q1'].astype(f32) * lp['lambda_k1'].astype(f32)))
            - jnp.exp(jnp.sum(lp['lambda_q2'].astype(f32) * lp['lambda_k2'].astype(f32))) + lam_init)

def layer_output(x, o_branches, g_n, z_n, o_d, z_d, lam_init, lp):
    B, T = x.shape[:2]
    o_nsa = jnp.sum(o_branches * g_n[..., None], axis=2).reshape(B, T, NSA_WIDTH)
    o_d = (rms_norm(o_d, lp['diff_out_norm']) * (1.0 - lam_init)).reshape(B, T, DIFF_WIDTH)
    o = jnp.concatenate([o_nsa * jax.nn.silu(z_n), o_d * jax.nn.silu(z_d)], axis=-1)
    return x + o @ lp['w_out']

def prompt_layer(x, lp, lam_init):
    B, T, _ = x.shape
    pos = jnp.arange(T)
    q_n, kv_c, kv_s, kv_w, g_n, z_n, q_d, k_d, v_d, z_d = project(x, pos, lp)
    kc, vc, cend = compressed_kv(kv_c, lp)
    kv_sel = pad_to_multiple(kv_s, SEL_BLOCK)
    overlap = selection_overlap(kc.shape[1], kv_sel.shape[1] // SEL_BLOCK)
    kv_w_pad = jnp.pad(kv_w, ((0, 0), (WINDOW, 0), (0, 0), (0, 0), (0, 0)))

    def nsa_block(i):
        s0 = i * NSA_Q_BLOCK
        qb = lax.dynamic_slice_in_dim(q_n, s0, NSA_Q_BLOCK, axis=1)
        qpos = s0 + jnp.arange(NSA_Q_BLOCK)
        o_c, o_s = nsa_cmp_sel(qb, qpos, kc, vc, cend, kv_sel[:, :, 0], kv_sel[:, :, 1], overlap)
        kvw = lax.dynamic_slice_in_dim(kv_w_pad, s0, WINDOW + NSA_Q_BLOCK, axis=1)
        kpos = s0 - WINDOW + jnp.arange(WINDOW + NSA_Q_BLOCK)
        o_w = window_attend(qb, kvw[:, :, 0], kvw[:, :, 1], qpos, kpos)
        return jnp.stack([o_c, o_s, o_w], axis=2)

    o_n = lax.map(nsa_block, jnp.arange(T // NSA_Q_BLOCK))
    o_n = jnp.moveaxis(o_n, 0, 1).reshape((B, T) + o_n.shape[3:])

    lam = diff_lambda(lp, lam_init)

    def diff_block(i):
        s0 = i * Q_BLOCK
        qb = lax.dynamic_slice_in_dim(q_d, s0, Q_BLOCK, axis=1)
        return diff_attend(qb, k_d, v_d, s0 + jnp.arange(Q_BLOCK), pos, lam)

    o_d = lax.map(diff_block, jnp.arange(T // Q_BLOCK))
    o_d = jnp.moveaxis(o_d, 0, 1).reshape(B, T, DIFF_HEADS, DIFF_V_DIM)
    y = layer_output(x, o_n, g_n, z_n, o_d, z_d, lam_init, lp)
    return y, (kv_c, kv_s, kv_w[:, T - min(WINDOW, T):], k_d, v_d)

def sample_layer(x, cache_c, cache_s, cache_dk, cache_dv, win, page_table, lp, lam_init):
    DB, T, _ = x.shape
    past = page_table.shape[1] * cache_c.shape[1]
    pos = past + jnp.arange(T)
    q_n, kv_c, kv_s, kv_w, g_n, z_n, q_d, k_d, v_d, z_d = project(x, pos, lp)

    def gather(pool):
        return pool[page_table].reshape((DB, past) + pool.shape[2:])

    kc, vc, cend = compressed_kv(jnp.concatenate([gather(cache_c), kv_c], axis=1), lp)
    kv_sel = pad_to_multiple(jnp.concatenate([gather(cache_s), kv_s], axis=1), SEL_BLOCK)
    overlap = selection_overlap(kc.shape[1], kv_sel.shape[1] // SEL_BLOCK)
    o_c, o_s = nsa_cmp_sel(q_n, pos, kc, vc, cend, kv_sel[:, :, 0], kv_sel[:, :, 1], overlap)
    w_buf = win.shape[1]
    win_all = jnp.concatenate([win, kv_w], axis=1)
    kpos_w = past - w_buf + jnp.arange(w_buf + T)
    o_w = window_attend(q_n, win_all[:, :, 0], win_all[:, :, 1], pos, kpos_w)
    o_n = jnp.stack([o_c, o_s, o_w], axis=2)
    lam = diff_lambda(lp, lam_init)
    k_all = jnp.concatenate([gather(cache_dk), k_d], axis=1)
    v_all = jnp.concatenate([gather(cache_dv), v_d], axis=1)
    o_d = diff_attend(q_d, k_all, v_all, pos, jnp.arange(past + T), lam)
    y = layer_output(x, o_n, g_n, z_n, o_d, z_d, lam_init, lp)
    return y, (kv_c, kv_s, win_all[:, T:], k_d, v_d)

def setup_inputs(seed: int = 0) -> dict:
    key = jax.random.key(seed)
    k = jax.random.split(key, 32)
    n_pages = PAST_LEN // PAGE_SIZE
    n_used = DEC_BATCH * n_pages
    n_pool = n_used + n_used // 4
    w_buf = min(WINDOW, PAST_LEN)

    def normal(kk, shape, scale=1.0):
        return jax.random.normal(kk, shape, jnp.float32) * scale

    def gain(kk, dim):
        return 1.0 + normal(kk, (DEPTH, dim), 0.05)

    page_table = jax.random.permutation(k[0], n_pool)[:n_used].reshape(DEC_BATCH, n_pages).astype(jnp.int32)
    return {
        'x_prompt': normal(k[1], (BATCH, SEQ, D_MODEL)),
        'x_sample': normal(k[2], (DEC_BATCH, DEC_SEQ, D_MODEL)),
        'cache_nsa_cmp_kv': normal(k[3], (DEPTH, n_pool, PAGE_SIZE, 2, NSA_KV_HEADS, HEAD_DIM)),
        'cache_nsa_sel_kv': normal(k[4], (DEPTH, n_pool, PAGE_SIZE, 2, NSA_KV_HEADS, HEAD_DIM)),
        'cache_diff_k': normal(k[5], (DEPTH, n_pool, PAGE_SIZE, DIFF_HEADS, 2, DIFF_QK_DIM)),
        'cache_diff_v': normal(k[6], (DEPTH, n_pool, PAGE_SIZE, DIFF_HEADS, DIFF_V_DIM)),
        'state_nsa_win_kv': normal(k[7], (DEPTH, DEC_BATCH, w_buf, 2, NSA_KV_HEADS, HEAD_DIM)),
        'page_table': page_table,
        'norm_w': gain(k[8], D_MODEL),
        'w_in': normal(k[9], (DEPTH, D_MODEL, PROJ_COLS), D_MODEL ** -0.5),
        'nsa_q_norm': gain(k[10], HEAD_DIM),
        'nsa_kc_norm': gain(k[11], HEAD_DIM),
        'nsa_ks_norm': gain(k[12], HEAD_DIM),
        'nsa_kw_norm': gain(k[13], HEAD_DIM),
        'cmp_pos_k': normal(k[14], (DEPTH, CMP_BLOCK, HEAD_DIM), 0.1),
        'cmp_w1_k': normal(k[15], (DEPTH, CMP_BLOCK, HEAD_DIM, HEAD_DIM), (CMP_BLOCK * HEAD_DIM) ** -0.5),
        'cmp_w2_k': normal(k[16], (DEPTH, HEAD_DIM, HEAD_DIM), HEAD_DIM ** -0.5),
        'cmp_pos_v': normal(k[17], (DEPTH, CMP_BLOCK, HEAD_DIM), 0.1),
        'cmp_w1_v': normal(k[18], (DEPTH, CMP_BLOCK, HEAD_DIM, HEAD_DIM), (CMP_BLOCK * HEAD_DIM) ** -0.5),
        'cmp_w2_v': normal(k[19], (DEPTH, HEAD_DIM, HEAD_DIM), HEAD_DIM ** -0.5),
        'diff_q_norm': gain(k[20], DIFF_QK_DIM),
        'diff_k_norm': gain(k[21], DIFF_QK_DIM),
        'lambda_q1': normal(k[22], (DEPTH, DIFF_QK_DIM), 0.1),
        'lambda_k1': normal(k[23], (DEPTH, DIFF_QK_DIM), 0.1),
        'lambda_q2': normal(k[24], (DEPTH, DIFF_QK_DIM), 0.1),
        'lambda_k2': normal(k[25], (DEPTH, DIFF_QK_DIM), 0.1),
        'diff_out_norm': gain(k[26], DIFF_V_DIM),
        'w_out': normal(k[27], (DEPTH, MIX_WIDTH, D_MODEL), MIX_WIDTH ** -0.5),
    }

def reference(x_prompt, x_sample, cache_nsa_cmp_kv, cache_nsa_sel_kv, cache_diff_k, cache_diff_v,
              state_nsa_win_kv, page_table, norm_w, w_in, nsa_q_norm, nsa_kc_norm, nsa_ks_norm,
              nsa_kw_norm, cmp_pos_k, cmp_w1_k, cmp_w2_k, cmp_pos_v, cmp_w1_v, cmp_w2_v,
              diff_q_norm, diff_k_norm, lambda_q1, lambda_k1, lambda_q2, lambda_k2, diff_out_norm, w_out):
    y_p, y_s = x_prompt, x_sample
    p_states, s_states = [], []
    for layer in range(DEPTH):
        lp = {
            'norm_w': norm_w[layer], 'w_in': w_in[layer],
            'nsa_q_norm': nsa_q_norm[layer], 'nsa_kc_norm': nsa_kc_norm[layer],
            'nsa_ks_norm': nsa_ks_norm[layer], 'nsa_kw_norm': nsa_kw_norm[layer],
            'cmp_pos_k': cmp_pos_k[layer], 'cmp_w1_k': cmp_w1_k[layer], 'cmp_w2_k': cmp_w2_k[layer],
            'cmp_pos_v': cmp_pos_v[layer], 'cmp_w1_v': cmp_w1_v[layer], 'cmp_w2_v': cmp_w2_v[layer],
            'diff_q_norm': diff_q_norm[layer], 'diff_k_norm': diff_k_norm[layer],
            'lambda_q1': lambda_q1[layer], 'lambda_k1': lambda_k1[layer],
            'lambda_q2': lambda_q2[layer], 'lambda_k2': lambda_k2[layer],
            'diff_out_norm': diff_out_norm[layer], 'w_out': w_out[layer],
        }
        lam_init = 0.8 - 0.6 * math.exp(-0.3 * layer)
        y_p, ps = prompt_layer(y_p, lp, lam_init)
        y_s, ss = sample_layer(y_s, cache_nsa_cmp_kv[layer], cache_nsa_sel_kv[layer], cache_diff_k[layer],
                               cache_diff_v[layer], state_nsa_win_kv[layer], page_table, lp, lam_init)
        p_states.append(ps)
        s_states.append(ss)
    p_c, p_s, p_w, p_dk, p_dv = [jnp.stack(t, axis=0) for t in zip(*p_states)]
    s_c, s_s, s_w, s_dk, s_dv = [jnp.stack(t, axis=0) for t in zip(*s_states)]
    return (y_p, y_s, p_c, p_s, p_w, p_dk, p_dv, s_c, s_s, s_w, s_dk, s_dv)


_drawn_inputs = setup_inputs


def setup_inputs(seed=0):
    import zlib

    import numpy as np

    out = dict(_drawn_inputs(seed))
    spreads = {}
    factors = {'cache_nsa_cmp_kv': 4.25,
     'cache_nsa_sel_kv': 5.244,
     'nsa_q_norm': 8.0,
     'nsa_kc_norm': 8.0,
     'cmp_pos_k': 8.0,
     'cmp_pos_v': 6.931,
     'diff_q_norm': 2.87,
     'lambda_q1': 5.719,
     'lambda_k1': 8.0,
     'lambda_q2': 4.903,
     'diff_out_norm': 3.756}
    for name, (base, spread) in spreads.items():
        noise = np.random.default_rng([zlib.crc32(name.encode()), seed]).standard_normal(out[name].shape)
        drawn = base * np.exp(spread * noise) if base else spread * noise
        out[name] = jnp.asarray(drawn.astype(out[name].dtype))
    for name, factor in factors.items():
        out[name] = (out[name] * factor).astype(out[name].dtype)
    return out
```

```python
import numpy as np
import concourse.bass as bass
from concourse import mybir
from contextlib import ExitStack

F32 = mybir.dt.float32
I32 = mybir.dt.int32
ALU = mybir.AluOpType
ACT = mybir.ActivationFunctionType
AX = mybir.AxisListType

P = 128
D_MODEL, SEQ, DEC = 1024, 512, 8
PAST, PAGE, N_POOL = 4096, 128, 320
PAGES = PAST // PAGE
HD, NH, NKV, GRP = 64, 8, 2, 4
DH, DQ, DV = 8, 32, 64
KC = D_MODEL // P
TILES = SEQ // P
CHUNK, NCHUNK = 512, 8
COLS = CHUNK * NCHUNK
LP = 8
UNITS = PAST // 16
NCMP = UNITS - 1
P_UNITS = SEQ // 16
P_NCMP = P_UNITS - 1
N_CAND = 62
N_TOP = 13
SP_SLOTS = 8
EPS = 1e-6
NEG = -1e30
LAM_INIT = 0.8 - 0.6
Q_SCALE_N, Q_SCALE_D = HD ** -0.5, DQ ** -0.5

C_QD, C_KD, C_VD, C_QN = 0, 512, 1024, 1536
C_KS, C_KW, C_VS, C_VW = 2048, 2176, 2304, 2432
C_KVC, C_G, C_ZN, C_ZD = 2560, 2816, 3072, 3584
N_NORM32, N_NORM64 = 32, 12
N_STAT = N_NORM32 + N_NORM64


CONST_COLS = {}


def const_table():
    parts = {}
    parts["ident"] = np.eye(P, dtype=np.float32)

    def rotary(pos, half):
        inv = np.float32(500000.0) ** (-np.arange(half, dtype=np.float32) / np.float32(half))
        ang = pos.astype(np.float32)[:, None] * inv.astype(np.float32)
        c, s = np.cos(ang), np.sin(ang)
        return np.concatenate([c, c, -s, s], axis=1).astype(np.float32)

    rope = []
    for t in range(TILES + 1):
        pos = np.arange(P) + P * t if t < TILES else np.full(P, PAST)
        rope += [rotary(pos, 8), rotary(pos, 4)]
    parts["rope"] = np.concatenate(rope, axis=1)
    parts["ropec"] = np.concatenate([rotary((np.arange(P) + P * n) * 16 + 31, 8) for n in range(2)], axis=1)
    q, k = np.arange(P)[:, None], np.arange(P)[None, :]
    parts["causal"] = np.where(k <= q, 0.0, NEG)
    n = np.arange(P_UNITS)[None, :]
    parts["cmp01"] = np.concatenate([((16 * n + 31 <= P * t + q) & (n < P_NCMP)) * 1.0 for t in range(TILES)], axis=1)
    parts["cmpneg"] = (parts["cmp01"] - 1.0) * -NEG
    cs, ss = np.arange(2 * P)[:, None] * 16, np.arange(65)[None, :] * 64
    ov = np.clip(np.minimum(cs + 32, ss + 64) - np.maximum(cs, ss), 0, None) / 16.0
    ov = ov[:, 1:1 + N_CAND]
    ov = np.concatenate([ov, ov[:, ::-1]], axis=1).reshape(2, P, 2 * N_CAND)
    parts["overlap"] = ov.transpose(1, 0, 2).reshape(P, 4 * N_CAND)
    row = np.arange(P)
    par = (row // 4) % 2
    sel = np.where(par[:, None] * (np.arange(64)[None, :] > 0) > 0, NEG, 0.0)
    parts["selmask"] = sel
    parts["pair"] = ((row[:, None] // 8 == row[None, :] // 8) & (row[:, None] % 4 == row[None, :] % 4)) * 1.0
    j, b, hp, c = row // 32, (row % 32) // 4, (row % 4) // 2, row % 2
    head = 2 * j + hp
    parts["dmap"] = (8 * b + head)[:, None] == np.arange(64)[None, :]
    parts["e12"] = np.stack([c == 0, c == 1], axis=1)
    parts["bmap"] = b[:, None] == np.arange(8)[None, :]
    parts["hmap"] = head[:, None] == np.arange(8)[None, :]
    parts["diag"] = (((row % 32) // 8)[:, None, None] == np.arange(4)[None, :, None]) & \
        ((row % 8)[:, None, None] == np.arange(8)[None, None, :])
    parts["diag"] = parts["diag"].reshape(P, 32)
    parts["iota64"] = (row % 64)[:, None]
    parts["later"] = np.broadcast_to(np.arange(124)[None, :] > N_CAND - 1, (P, 124))
    parts["slots"] = np.broadcast_to(np.arange(N_TOP)[None, :], (P, N_TOP))
    parts["eye16"] = row[:, None] == np.arange(16)[None, :]
    half = np.arange(64) % 2
    parts["blockrow"] = 2 * half[None, :] + (row % 2)[:, None]
    at, cols = 0, []
    for name, a in parts.items():
        a = np.asarray(a, np.float32)
        CONST_COLS[name] = (at, a.shape[1])
        at += a.shape[1]
        cols.append(a)
    return np.ascontiguousarray(np.concatenate(cols, axis=1))


def laid_out(x):
    f = np.ascontiguousarray
    z = np.zeros
    n_pool = x["cache_nsa_cmp_kv"].shape[1]

    def by_rgd(a):
        return a.reshape(a.shape[:-1] + (NKV, GRP, -1)).swapaxes(-3, -2).reshape(a.shape)

    xs = np.concatenate([x["x_prompt"][0], x["x_sample"][:, 0]], axis=0)
    w = x["w_in"][0]
    cut = np.cumsum([512, 256, 256, 256, 24, 512, 512, 512, 512, 512])[:-1]
    q_n, kv_c, kv_s, kv_w, g_n, z_n, q_d, k_d, v_d, z_d = np.split(w, cut, axis=1)
    g_n = g_n.reshape(D_MODEL, 3, NKV, GRP).swapaxes(2, 3).reshape(D_MODEL, 24)
    w = np.concatenate([q_d, k_d, v_d, by_rgd(q_n), kv_s[:, :P], kv_w[:, :P], kv_s[:, P:], kv_w[:, P:],
                        kv_c, g_n, z((D_MODEL, 232), w.dtype), by_rgd(z_n), z_d], axis=1)
    w_out = x["w_out"][0]
    w_out = np.concatenate([by_rgd(w_out[:512].T).T, w_out[512:]], axis=0)
    w1 = np.stack([x["cmp_w1_k"][0], x["cmp_w1_v"][0]])
    pos = np.stack([x["cmp_pos_k"][0], x["cmp_pos_v"][0]])
    w2 = np.stack([x["cmp_w2_k"][0], x["cmp_w2_v"][0]])
    w2b = z((2, 2, 64, 2, 64), w2.dtype)
    w2b[:, 0, :, 0], w2b[:, 1, :, 1] = w2, w2
    cmp_kv = x["cache_nsa_cmp_kv"][0].reshape(n_pool, 8, LP, 2, 2, NKV, HD)
    sel = x["cache_nsa_sel_kv"][0].reshape(n_pool, 2, 64, 2, NKV, HD)
    sel = np.stack([sel[:, :, :, 0].transpose(0, 1, 3, 4, 2), sel[:, :, :, 1].transpose(0, 1, 3, 2, 4)], axis=4)
    dk = x["cache_diff_k"][0].reshape(n_pool, PAGE, 4, P)
    win = x["state_nsa_win_kv"][0]
    row = [x["diff_q_norm"][0], x["diff_k_norm"][0], x["nsa_q_norm"][0], x["nsa_ks_norm"][0], x["nsa_kw_norm"][0],
           x["nsa_kc_norm"][0], x["diff_out_norm"][0], x["lambda_q1"][0], x["lambda_k1"][0], x["lambda_q2"][0],
           x["lambda_k2"][0]]
    return {
        "consts": const_table(),
        "params": f(np.concatenate(row)[None, :]),
        "norm_w": f(x["norm_w"][0].reshape(KC, P).T),
        "x_nat": f(xs),
        "x_t": f(xs.T.reshape(KC, P, SEQ + DEC).transpose(1, 0, 2)),
        "w_in": f(w.reshape(KC, P, NCHUNK, CHUNK).transpose(2, 1, 0, 3).reshape(NCHUNK, P, KC * CHUNK)),
        "w_out": f(w_out.reshape(KC, P, D_MODEL).transpose(1, 0, 2)),
        "w1": f(w1.reshape(2, 2, LP, 2, HD, HD).transpose(3, 4, 0, 1, 2, 5).reshape(P, 2, 2, LP, HD)),
        "cmp_pos": f(pos.reshape(2, 2, LP, 2, HD).transpose(3, 4, 0, 1, 2).reshape(P, 2, 2, LP)),
        "w2": f(w2b.transpose(1, 2, 0, 3, 4).reshape(P, 2, P)),
        "cmp_cache": f(cmp_kv.transpose(0, 3, 6, 1, 4, 5, 2).reshape(n_pool, P, 256)),
        "sel_cache": f(sel.reshape(n_pool * 2 * NKV * 64, P)),
        "dk_cache": f(dk.transpose(0, 3, 2, 1).reshape(n_pool, P, 512)),
        "dv_cache": f(x["cache_diff_v"][0].reshape(n_pool, PAGE, 512)),
        "win_kt": f(win[:, :, 0].reshape(DEC, SEQ, P).transpose(2, 0, 1)),
        "win_v": f(win[:, :, 1].reshape(DEC, 4, P, P).transpose(2, 0, 1, 3)),
        "win_nat": f(win.reshape(DEC, SEQ, 256)),
        "pages": f(x["page_table"].astype(np.int32).reshape(1, DEC * PAGES)),
        "pages_bg": f(np.repeat(x["page_table"].astype(np.int32), NKV, axis=0)),
    }


def program(nc, src, dst):
    ctx = ExitStack()
    with ctx:
        def sb(name, shape, dt=F32):
            return ctx.enter_context(nc.sbuf_tensor(name, shape, dt))

        def sem(name):
            return ctx.enter_context(nc.semaphore(name))

        consts = sb("consts", [P, src["consts"].shape[1]])
        params = sb("params", [P, 512])
        norm_w = sb("norm_w", [P, KC])
        w2 = sb("w2", [P, 2, P])
        pages = sb("pages", [1, DEC * PAGES], I32)
        stats = sb("stats", [P, TILES + 1, N_STAT])
        kc_stats = sb("kc_stats", [P, 34])
        x_rs = sb("x_rs", [P, TILES + 1])
        small = sb("small", [P, 64])
        bias = sb("bias", [P, 2, 2])
        q_nsa = sb("q_nsa", [P, DEC, 64])
        q_sel = sb("q_sel", [P, 16, 32])
        k_new = sb("k_new", [P, 6, DEC])
        index = sb("index", [P, P], I32)
        sample = sb("sample", [DEC, COLS])
        o_parts = sb("o_parts", [P, 3, DEC, GRP])
        o_diff = sb("o_diff", [P, 4, DEC])
        spread = sb("spread", [P, 256])
        pages_bg = sb("pages_bg", [16, PAGES], I32)
        ones = sb("ones", [P, 64])
        work = sb("work", [P, 160])
        proj = sb("proj", [P, TILES, COLS])
        ring = sb("ring", [P, 16384])
        wide = sb("wide", [P, 4104])
        xt = sb("xt", [P, KC, SEQ + DEC])
        xn = sb("xn", [P, 4096])
        small8 = sb("small8", [P, 2048])
        banks = ctx.enter_context(nc.psum_tensor("banks", [P, 8, 512], F32))

        xt_flat = xt[:, :, :].rearrange("p k n -> p (k n)")

        def const(name):
            at, n = CONST_COLS[name]
            return consts[:, at:at + n]

        d_weights, own_rows, own_weights = work[:, 0:64], work[:, 64:72], work[:, 72:80]
        lam_work = work[:, 80:144]
        ident = const("ident")
        rope = const("rope").rearrange("p (t n) -> p t n", t=TILES + 1)
        ropec = const("ropec").rearrange("p (t n) -> p t n", t=2)
        cmp_rows = proj[:, :, :].rearrange("p t n -> p (t n)").rearrange("p (u g n) -> p u g n", u=2, g=PAGES)
        k_ring = ring[:, 0:8192].rearrange("p (s g n) -> p s g n", s=4, g=4)
        w_ring = ring[:, 8192:16384].rearrange("p (s k n) -> p s k n", s=2, k=KC)
        sel_kv = ring[:, 8192:16384].rearrange("p (q s n) -> p q s n", q=8, s=SP_SLOTS)
        x_tok = ring[:, 0:4096].rearrange("p (t n) -> p t n", t=TILES)
        x_new = ring[0:DEC, 4096:5120]
        w1 = wide[:, 0:2048].rearrange("p (k h l e) -> p k h l e", k=2, h=2, l=LP)
        hid = wide[:, 2048:3072].rearrange("p (u k n) -> p u k n", u=2, k=2)
        sig = wide[:, 3072:4096].rearrange("p (u k n) -> p u k n", u=2, k=2)
        cmp_pos = small8[:, 0:32].rearrange("p (k h l) -> p k h l", k=2, h=2)
        kc_t = wide[:, 0:2048].rearrange("p (b n) -> p b n", b=DEC)
        kc_n = xn[:, 0:2048].rearrange("p (b n) -> p b n", b=DEC)
        vc_n = xn[:, 2048:4096].rearrange("p (b n) -> p b n", b=DEC)
        q_blk = small8[:, 0:1024].rearrange("p (j b n) -> p j b n", j=4, b=DEC)
        scores = wide[:, 0:PAST + 1]

        p_cmp = wide[0:64, 2048:2304]
        p_cmp_t = wide[:, 2304:2432].rearrange("p (n m) -> p n m", n=2)
        group_p = wide[:, 2432:2464].rearrange("p (n m) -> p n m", n=2)
        imp = wide[0:16, 2464:2464 + 2 * N_CAND]
        rank, rank2 = wide[0:16, 2600:2662], wide[0:16, 2662:2724]
        block_row_flat = wide[0:16, 2724:2788]
        block_row = block_row_flat.rearrange("p (g h) -> p g h", h=2)
        slot_row = wide[0:16, 2788:2804]
        own_a = small[0:DEC, 40:48]
        gates, new_gates = proj[:, :, C_G:C_G + 24], sample[:, C_G:C_G + 24]
        gates_by_head = gates.rearrange("p t (b h) -> p t b h", b=3)
        out_stats = stats[:, :, 0:DH]

        def z_exp(t):
            return proj[:, t, 1024:2048] if t < TILES else sample[:, 1024:2048]

        p_win = xt_flat[0:64, 3072:3584]
        p_win_t = xt_flat[:, 3584:3840].rearrange("p (k m) -> p k m", k=4)
        n_pt = xt_flat[:, 3072:4096].rearrange("p (c n) -> p c n", c=2)
        q_pad = xn[:, 0:3072].rearrange("p (q n) -> p q n", q=6)
        d_pt = xn[:, 3072:3584]
        p_pct = xn[0:32, 3584:3712]
        e_bufs = proj[:, :, 1536:2048]
        v_masked = proj[:, 0:2, 2048:2304]
        p_kc, p_vc = proj[0:32, 2, 2048:2176], proj[0:32, 2, 2176:2304]
        p_kc_t = proj[:, 3, 2048:2080]
        p_hid = proj[:, 3, 2080:2144].rearrange("p (k n) -> p k n", k=2)
        p_sig = proj[:, 3, 2144:2208].rearrange("p (k n) -> p k n", k=2)
        p_pc = proj[:, 3, 2208:2240]
        p_sel = q_nsa[0:64, :, :].rearrange("p b n -> p (b n)")
        p_sel_t = spread[:, :].rearrange("p (m n) -> p m n", m=SP_SLOTS)
        sel_line = work[0:1, 80:144]

        S = {}

        def s(name):
            if name not in S:
                S[name] = sem(name)
            return S[name]

        class Chain:

            def __init__(self, eng, name):
                self.eng, self.sem, self.n, self.base = eng, s(name), 0, 0

            def link(self, ins):
                self.n += 1
                ins.then_inc(self.sem, 1)
                self.eng.wait_ge(self.sem, self.base + self.n)

            def loop(self, i, per):
                self.start = self.n
                self.base = i * per

            def end(self, times, per):
                assert self.n - self.start == per, (self.n - self.start, per)
                self.n, self.base = self.start + times * per, 0

        def bc(ap, n, at):
            return ap.unsqueeze(at).broadcast_to(list(ap.shape[:at]) + [n] + list(ap.shape[at:]))

        win_kt = xn[:, :].rearrange("p (b n) -> p b n", b=DEC)
        win_v = xn[:, :].rearrange("p (b k n) -> p b k n", b=DEC, k=4)
        w1_again = ring[:, 6144:8192].rearrange("p (k h l e) -> p k h l e", k=2, h=2, l=LP)
        probs_t = small8[:, :].rearrange("p (g n) -> p g n", g=PAGES)
        q_t = wide[:, 0:4096].rearrange("p (c n) -> p c n", c=8)
        k_t = xt_flat[:, 0:3072].rearrange("p (c n) -> p c n", c=6)
        p_rows = xt_flat[:, 3072:4096].rearrange("p (u n) -> p u n", u=P_UNITS)
        w_out = ring[:, 0:8192].rearrange("p (k n) -> p k n", k=KC)
        x_again = xn[:, :].rearrange("p (t n) -> p t n", t=TILES)
        x_new_again = small8[0:DEC, 0:1024]
        o_t = wide[:, 0:2048].rearrange("p (u k n) -> p u k n", u=2, k=KC)
        N_SETUP = 9
        N_STORES = 1 + TILES + 1
        block = ctx.enter_context(nc.Block())

        @block.sync
        def _(sp):
            def page_dma(cache, at, to, done):
                pg = sp.value_load(pages[0:1, bass.ds(at, 1)], min_val=0, max_val=N_POOL - 1)
                rows = cache[bass.ds(pg, 1), :, :].rearrange("o p n -> (o p) n")
                sp.dma_start(to, rows).then_inc(done, 16)

            sp.dma_start(pages[:, :], src["pages"][:, :]).then_inc(s("pages_in"), 16)
            sp.dma_start(w1, src["w1"][:, :, :, :, :]).then_inc(s("setup_in"), 16)
            sp.dma_start(cmp_pos, src["cmp_pos"][:, :, :, :]).then_inc(s("setup_in"), 16)
            sp.dma_start(w2[:, :, :], src["w2"][:, :, :]).then_inc(s("setup_in"), 16)
            sp.dma_start(consts[:, :], src["consts"][:, :]).then_inc(s("setup_in"), 16)
            sp.wait_ge(s("pages_in"), 16)

            def load_cmp(b, u):
                def load(g):
                    page_dma(src["cmp_cache"], b * PAGES + g, cmp_rows[:, u, bass.ds(g, 1), :].rearrange("p o n -> p (o n)"),
                             s(f"cmp_in{u}"))

                load(0)
                with sp.Fori(1, PAGES) as g:
                    load(g)

            load_cmp(0, 0)
            sp.dma_start(params[:, :], src["params"][:, :].partition_broadcast(P).rearrange("p o n -> p (o n)")).then_inc(s("setup_in"), 16)
            sp.dma_start(norm_w[:, :], src["norm_w"][:, :]).then_inc(s("setup_in"), 16)
            sp.dma_start(xt[:, :, :], src["x_t"][:, :, :]).then_inc(s("setup_in"), 16)
            sp.dma_start(x_tok, src["x_nat"][0:SEQ, :].rearrange("(t p) n -> p t n", p=P)).then_inc(s("setup_in"), 16)
            sp.dma_start(x_new, src["x_nat"][SEQ:SEQ + DEC, :]).then_inc(s("setup_in"), 16)
            for b in range(2):
                sp.dma_start(w_ring[:, b, :, :], src["w_in"][b, :, :].rearrange("p (k n) -> p k n", k=KC)).then_inc(s(f"w_in{b}"), 16)
                if b == 0:
                    load_cmp(1, 1)
            with sp.Fori(0, 3) as i:
                for u in range(2):
                    sp.wait_ge(s("pre_ready"), 2 * i + u + 1)
                    load_cmp(2 * i + 2 + u, u)
                    sp.wait_ge(s("new_proj_ready"), 2 * i + u + 1)
                    sp.dma_start(w_ring[:, u, :, :],
                                 src["w_in"][bass.ds(2 * i + 2 + u, 1), :, :].rearrange("o p (k n) -> p (o k) n", k=KC)
                                 ).then_inc(s(f"w_in{u}"), 16)

            sp.wait_ge(s("x_squared"), 1)
            def load_k(i, b):
                for g in range(4):
                    page_dma(src["dk_cache"], b * PAGES + 4 * i + g, k_ring[:, b % 4, g, :], s(f"k_in{b % 4}"))

            def load_w(i, u):
                sp.dma_start(w_ring[:, u, :, :],
                             src["w_in"][bass.ds(2 * i + u, 1), :, :].rearrange("o p (k n) -> p (o k) n", k=KC)
                             ).then_inc(s(f"w_in{u}"), 16)

            for b in range(4):
                load_k(0, b)
            for u in range(2):
                sp.wait_ge(s("new_proj_ready"), 7 + u)
                load_w(0, u)
            for b in range(4, 8):
                sp.wait_ge(s("k_used"), b - 3)
                load_k(0, b)
            with sp.Fori(0, 3) as i:
                for u in range(2):
                    for b in range(8):
                        sp.wait_ge(s("k_used"), 16 * i + 8 * u + 8 + b - 3)
                        load_k(2 * i + u + 1, b)
                    sp.wait_ge(s("proj_ready"), 8 * i + 4 * u + 4)
                    load_w(i + 1, u)
            for b in range(8):
                sp.wait_ge(s("k_used"), 56 + b - 3)
                load_k(7, b)

            sp.wait_ge(s("ranked"), 1)
            sp.dma_start(win_kt, src["win_kt"][:, :, :]).then_inc(s("win_in"), 16)
            sp.wait_ge(s("k_used"), 64)
            sp.dma_start(w1_again, src["w1"][:, :, :, :, :]).then_inc(s("w1_in"), 16)

            def load_v(b, st, slot):
                for g in range(4):
                    page_dma(src["dv_cache"], b * PAGES + 4 * st + g, k_ring[:, slot, g, :], s(f"v_in{slot}"))

            for st in range(3):
                load_v(0, st, st)
            sp.wait_ge(s("norm_done"), 1)
            for name, cols, n in (("p_cmp", C_KVC, 256), ("p_dk", C_KD, 512), ("p_dv", C_VD, 512)):
                sp.dma_start(dst[name][:, :].rearrange("(t p) n -> p t n", p=P), proj[:, :, cols:cols + n]).then_inc(s("p_stored"), 16)
            for name, k_cols, v_cols in (("p_sel", C_KS, C_VS), ("p_win", C_KW, C_VW)):
                for c, at in ((0, k_cols), (P, v_cols)):
                    sp.dma_start(dst[name][:, c:c + P].rearrange("(t p) n -> p t n", p=P), proj[:, :, at:at + P]).then_inc(s("p_stored"), 16)
            for name, cols, n in (("s_cmp", C_KVC, 256), ("s_dk", C_KD, 512), ("s_dv", C_VD, 512)):
                sp.dma_start(dst[name][:, :], sample[:, cols:cols + n]).then_inc(s("s_stored"), 16)
            for c, at in ((0, C_KS), (P, C_VS)):
                sp.dma_start(dst["s_sel"][:, c:c + P], sample[:, at:at + P]).then_inc(s("s_stored"), 16)
            for c, at in ((0, C_KW), (P, C_VW)):
                sp.dma_start(dst["s_win"][:, SEQ - 1, c:c + P], sample[:, at:at + P]).then_inc(s("s_stored"), 16)
            sp.dma_start(dst["s_win"][:, 0:SEQ - 1, :].rearrange("b (s k) n -> b s (k n)", s=7),
                         src["win_nat"][:, 1:SEQ, :].rearrange("b (s k) n -> b s (k n)", s=7)).then_inc(s("stored"), 16)
            sp.wait_ge(s("win_scored"), 1)
            sp.dma_start(win_v, src["win_v"][:, :, :, :]).then_inc(s("win_in"), 16)
            sp.wait_ge(s("win_in"), 32)
            for b in range(DEC):
                sp.dma_start(win_v[0:1, b, 0, :], sample[b:b + 1, C_VW:C_VW + P]).then_inc(s("win_new_in"), 16)

            sp.wait_ge(s("p_compressed"), 1)
            load_v(0, 3, 3)
            for st in range(4, 8):
                sp.wait_ge(s("v_used"), st - 3)
                load_v(0, st, st % 4)
            with sp.Fori(0, DEC - 1) as b:
                for st in range(8):
                    sp.wait_ge(s("v_used"), 8 * b + 8 + st - 3)
                    load_v(b + 1, st, st % 4)

            sp.wait_ge(s("v_used"), 64)
            sp.dma_start(w_out, src["w_out"][:, :, :]).then_inc(s("w_out_in"), 16)
            sp.wait_ge(s("attended"), 1)
            sp.dma_start(x_again, src["x_nat"][0:SEQ, :].rearrange("(t p) n -> p t n", p=P)).then_inc(s("x_in"), 16)
            sp.dma_start(x_new_again, src["x_nat"][SEQ:SEQ + DEC, :]).then_inc(s("x_in"), 16)
            for t in range(TILES):
                sp.wait_ge(s("y_ready"), t + 1)
                sp.dma_start(dst["y_p"][t * P:(t + 1) * P, :], proj[:, t, 1024:2048]).then_inc(s("stored"), 16)
            sp.wait_ge(s("y_ready"), TILES + 1)
            sp.dma_start(dst["y_s"][:, :], sample[:, 0:1024]).then_inc(s("stored"), 16)
            sp.wait_ge(s("stored"), 16 * N_STORES)

        @block.tensor
        def _(pe):
            mm, tr = nc.tensor.matmul, nc.tensor.transpose

            pe.wait_ge(s("setup_in"), 16 * N_SETUP)
            for kv in range(2):
                for lh in range(2 * LP):
                    for g in range(2):
                        last = mm(banks[64 * g:64 * g + 64, 6, kv:kv + 1], w1[:, kv, lh // LP, lh % LP, :],
                                  cmp_pos[:, kv, lh // LP, lh % LP:lh % LP + 1],
                                  start=lh == 0, stop=lh == 2 * LP - 1, tile_position=(0, 64 * g))
            last.then_inc(s("bias_ready"), 1)

            def first_layer(turn, u):
                pe.wait_ge(s(f"cmp_in{u}"), 16 * PAGES * turn)
                rows = cmp_rows[:, u, :, :].rearrange("p g n -> p (g n)").rearrange("p (n k g l) -> p k g l n", k=2, g=2, l=LP)
                for kv in range(2):
                    for lp in range(LP):
                        for half in range(2):
                            for g in range(2):
                                last = mm(banks[64 * g:64 * g + 64, u, 256 * kv:256 * kv + NCMP], w1[:, kv, half, lp, :],
                                          rows[:, kv, g, lp, half:half + NCMP], start=lp + half == 0,
                                          stop=lp == LP - 1 and half == 1, tile_position=(0, 64 * g))
                last.then_inc(s("pre_ready"), 1)

            def new_projection(turn, u):
                pe.wait_ge(s(f"w_in{u}"), 16 * turn)
                for m in range(2):
                    for j in range(4):
                        last = mm(banks[32 * j:32 * j + DEC, 2 + u, :], xt[:, j + 4 * m, SEQ:SEQ + DEC],
                                  w_ring[:, u, j + 4 * m, :], start=m == 0, stop=m == 1, tile_position=(0, 32 * j))
                last.then_inc(s("new_proj_ready"), 1)

            def second_layer(u):
                for kv in range(2):
                    for nt in range(2):
                        last = mm(banks[:, 4 + u, 256 * kv + P * nt:256 * kv + P * nt + P], hid[:, u, kv, P * nt:P * nt + P],
                                  w2[:, kv, :], start=True, stop=True)
                last.then_inc(s("rows_ready"), 1)

            first_layer(1, 0)
            pe.wait_ge(s("x_scaled"), 1)
            new_projection(1, 0)
            first_layer(1, 1)
            pe.wait_ge(s("hid_ready"), 1)
            second_layer(0)
            new_projection(1, 1)
            with pe.Fori(0, 3) as i:
                for u in range(2):
                    pe.wait_ge(s("hid_ready"), 2 * i + u + 1)
                    first_layer(i + 2, u)
                    pe.wait_ge(s("hid_ready"), 2 * i + u + 2)
                    pe.wait_ge(s("rows_kept"), 2 * i + u + 1)
                    second_layer(1 - u)
                    pe.wait_ge(s("new_proj_used"), 2 * i + u + 1)
                    new_projection(i + 2, u)
            pe.wait_ge(s("hid_ready"), 8)
            pe.wait_ge(s("rows_kept"), 7)
            second_layer(1)

            pe.wait_ge(s("new_normed"), 1)
            cols = [C_QD + P * j for j in range(4)] + [C_QN + P * r for r in range(4)] + \
                   [C_KD + P * j for j in range(4)] + [C_KS, C_KW]
            for n, c in enumerate(cols):
                last = tr(banks[:, 6, 8 * n:8 * n + 8], sample[:, c:c + P], ident[0:DEC, 0:DEC])
            last.then_inc(s("new_turned"), 1)
            pe.wait_ge(s("kc_normed"), 1)
            pe.wait_ge(s("rows_kept"), 9)
            for b in range(DEC):
                for nt in range(2):
                    last = tr(banks[:, b // 2, 256 * (b % 2) + P * nt:256 * (b % 2) + P * nt + P], kc_n[:, b, P * nt:P * nt + P], ident)
                if b % 2:
                    last.then_inc(s("kc_turned"), 1)
            pe.wait_ge(s("q_placed"), 1)
            pe.wait_ge(s("kc_t_ready"), 4)
            for b in range(DEC):
                last = mm(banks[0:64, 7, 0:NCMP], q_nsa[:, b, :], kc_t[:, b, 0:NCMP], start=b == 0, stop=b == DEC - 1)
            last.then_inc(s("cmp_scored"), 1)
            for b in range(DEC):
                for j in range(4):
                    last = mm(banks[32 * j:32 * j + 32, 5, 0:1], q_blk[:, j, b, :], k_new[:, j, b:b + 1],
                              start=b == 0, stop=b == DEC - 1, tile_position=(0, 32 * j))
            last.then_inc(s("own_scored"), 1)
            pe.wait_ge(s("cmp_probs"), 1)
            for nt in range(2):
                last = tr(banks[:, 6, 256 + 64 * nt:256 + 64 * nt + 64], p_cmp[:, P * nt:P * nt + P], ident[0:64, 0:64])
            last.then_inc(s("cmp_probs_turned"), 1)
            pe.wait_ge(s("group_probs"), 1)
            for nt in range(2):
                last = mm(banks[0:16, 4, 0:2 * N_CAND], group_p[:, nt, :], const("overlap")[:, 124 * nt:124 * nt + 124],
                          start=nt == 0, stop=nt == 1)
            last.then_inc(s("importance"), 1)
            for b in range(DEC):
                for nt in range(2):
                    last = mm(banks[:, 3, 128 + 8 * b:136 + 8 * b], vc_n[:, b, P * nt:P * nt + P], p_cmp_t[:, nt, 8 * b:8 * b + 8],
                              start=nt == 0, stop=nt == 1)
            last.then_inc(s("cmp_out"), 1)

            def k_step(b, u, waited):
                pe.wait_ge(s(f"k_in{b % 4}"), waited)
                for j in range(4):
                    last = mm(banks[32 * j:32 * j + 32, u, :], q_blk[:, j, b, :],
                              k_ring[:, b % 4, :, P * j:P * j + P], start=b == 0, stop=b == DEC - 1,
                              tile_position=(0, 32 * j))
                last.then_inc(s("k_used"), 1)

            pe.wait_ge(s("own_kept"), 1)
            pe.wait_ge(s("cmp_out_kept"), 1)
            with pe.Fori(0, 4) as i:
                for u in range(2):
                    pe.wait_ge(s("scores_kept"), 2 * i + u + 1)
                    for b in range(DEC):
                        k_step(b, u, 64 * (4 * i + 2 * u + b // 4 + 1))
                        t = b // 2
                        if b == 0:
                            pe.wait_ge(s(f"w_in{u}"), 16 * (i + 5))
                        if b % 2 == 0:
                            pe.wait_ge(s("proj_kept"), 8 * i + 4 * u + t + 1)
                        for k in range(4 * (b % 2), 4 * (b % 2) + 4):
                            last = mm(banks[:, 2 + t, :], xt[:, k, P * t:P * t + P], w_ring[:, u, k, :],
                                      start=k == 0, stop=k == KC - 1)
                        if b % 2:
                            last.then_inc(s("proj_ready"), 1)

            pe.wait_ge(s("proj_kept"), 36)
            pe.wait_ge(s("rows_spread"), 1)
            for par in range(2):
                last = mm(banks[64 * par:64 * par + 64, 6, 0:P], ones[0:16, :], spread[0:16, P * par:P * par + P],
                          start=True, stop=True, tile_position=(0, 64 * par))
            last.then_inc(s("index_spread"), 1)
            pe.wait_ge(s("diff_weights"), 1)
            for g in range(PAGES):
                last = mm(banks[:, g // 8, 64 * (g % 8):64 * (g % 8) + 64], scores[:, P * g:P * g + P], d_weights,
                          start=True, stop=True)
                if g % 8 == 7:
                    last.then_inc(s("probs_turned"), 1)
            mm(banks[0:DEC, 4, 0:DH], own_rows, own_weights, start=True, stop=True).then_inc(s("own_weighted"), 1)
            pe.wait_ge(s("norm_done"), 1)
            pe.wait_ge(s("own_read"), 1)
            cols = [C_QD + P * j for j in range(4)] + [C_QN + P * r for r in range(4)] + \
                   [C_KD + P * j for j in range(4)] + [C_KS, C_KW, C_KVC, C_KVC + P]
            for n, c in enumerate(cols):
                if n < 4:
                    pe.wait_ge(s("probs_kept"), n + 1)
                else:
                    pe.wait_ge(s("turned_kept"), n - 3)
                for t in range(TILES):
                    last = tr(banks[:, n % 4, P * t:P * t + P], proj[:, t, c:c + P], ident)
                last.then_inc(s("turned"), 1)
            pe.wait_ge(s("turned_kept"), len(cols))
            pe.wait_ge(s("w1_in"), 16)
            for kv in range(2):
                for lp in range(LP):
                    for half in range(2):
                        for g in range(2):
                            last = mm(banks[64 * g:64 * g + 64, 4, 32 * kv:32 * kv + P_NCMP], w1_again[:, kv, half, lp, :],
                                      p_rows[:, half:half + P_NCMP, 16 * kv + 8 * g + lp], start=lp + half == 0,
                                      stop=lp == LP - 1 and half == 1, tile_position=(0, 64 * g))
            last.then_inc(s("p_compressed"), 1)
            pe.wait_ge(s("win_key_placed"), 1)
            for b in range(DEC):
                last = mm(banks[0:64, 0, :], q_nsa[:, b, :], win_kt[:, b, :], start=b == 0, stop=b == DEC - 1)
            last.then_inc(s("win_scored"), 1)
            pe.wait_ge(s("p_hid"), 1)
            for kv in range(2):
                last = mm(banks[0:32, 5, P * kv:P * kv + P], p_hid[:, kv, :], w2[:, kv, :], start=True, stop=True)
            last.then_inc(s("p_rows_ready"), 1)
            pe.wait_ge(s("win_probs"), 1)
            for kt in range(4):
                last = tr(banks[:, 1, 64 * kt:64 * kt + 64], p_win[:, P * kt:P * kt + P], ident[0:64, 0:64])
            last.then_inc(s("win_probs_turned"), 1)
            pe.wait_ge(s("p_kc_normed"), 1)
            tr(banks[:, 5, 256:288], p_kc, ident[0:32, 0:32]).then_inc(s("p_kc_turned"), 1)
            pe.wait_ge(s("win_probs_kept"), 1)
            pe.wait_ge(s("win_new_in"), 16 * DEC)
            for b in range(DEC):
                for kt in range(4):
                    last = mm(banks[:, 1, 256 + 8 * b:264 + 8 * b], win_v[:, b, kt, :], p_win_t[:, kt, 8 * b:8 * b + 8],
                              start=kt == 0, stop=kt == 3)
            last.then_inc(s("win_out"), 1)

            def v_step(bi, bq, st, turn):
                pe.wait_ge(s(f"v_in{st % 4}"), 64 * turn)
                for j in range(4):
                    last = mm(banks[32 * j:32 * j + 32, 7, :], probs_t[:, 4 * st + j, 32 * bq:32 * bq + 32],
                              k_ring[:, st % 4, j, :], start=st == 0, stop=st == 7, tile_position=(0, 32 * j))
                last.then_inc(s("v_used"), 1)

            def head_scores(r, par, t):
                n = P * (t + 1)
                yield
                for c in range(2):
                    last = mm(banks[:, c, 0:n], q_pad[:, 3 * par + c, P * t:P * t + P],
                              k_t[:, bass.ds(r, 1), 0:n].rearrange("p o n -> p (o n)"), start=True, stop=True)
                last.then_inc(s("d_scored"), 1)
                yield
                for c in range(2):
                    last = mm(banks[:, 2 + c, 0:n], q_pad[:, 3 * par + 2, P * t:P * t + P], k_t[:, 4 + c, 0:n], start=True, stop=True)
                last = mm(banks[:, 6, 480:512], q_pad[:, 3 * par + 2, P * t:P * t + P], p_kc_t, start=True, stop=True)
                last.then_inc(s("n_scored"), 1)

            def d_output(r, t):
                for k in range(t + 1):
                    last = tr(banks[:, 4, P * k:P * k + P], e_bufs[:, 0, P * k:P * k + P], ident)
                last.then_inc(s("d_turned"), 1)

            def d_values(r, t, turn):
                pe.wait_ge(s("d_turned_kept"), turn)
                for k in range(t + 1):
                    last = mm(banks[:, 4, 0:P], d_pt[:, P * k:P * k + P],
                              proj[:, k, bass.ds(C_VD + P * r, P)], start=k == 0, stop=k == t)
                last.then_inc(s("d_out"), 1)

            def n_output(t):
                for c in range(2):
                    for k in range(t + 1):
                        tr(banks[:, 4 + c, P * k:P * k + P], e_bufs[:, 2 + c, P * k:P * k + P], ident)
                tr(banks[0:32, 2, 0:P], p_pc, ident).then_inc(s("n_turned"), 1)

            def n_values(par, t, turn):
                pe.wait_ge(s("n_turned_kept"), turn)
                pe.wait_ge(s("c_turned_kept"), turn)
                for c, at in ((0, C_VS), (1, C_VW)):
                    for k in range(t + 1):
                        mm(banks[:, 5, P * c:P + P * c], n_pt[:, c, P * k:P * k + P], proj[:, k, at:at + P],
                           start=k == 0, stop=k == t)
                mm(banks[:, 5, 256:320], p_pct, p_vc[:, 64 * par:64 * par + 64], start=True, stop=True).then_inc(s("n_out"), 1)

            def attend_heads(h2, i):
                for par in range(2):
                    r = 2 * h2 + i
                    hh = 2 * r + par
                    pe.wait_ge(s("q_padded"), hh + 1)
                    for t in range(TILES):
                        u = hh * 4 + t + 1
                        if t == 0:
                            pe.wait_ge(s("v_masked"), hh + 1)
                        v_step(hh, h2, 2 * t, 2 * hh + t // 2 + 1)
                        pe.wait_ge(s("d_exps"), u)
                        both = head_scores(r, par, t)
                        next(both)
                        next(both)
                        if t > 0:
                            n_tail(par, t - 1, u - 1)
                        v_step(hh, h2, 2 * t + 1, 2 * hh + t // 2 + 1)
                        pe.wait_ge(s("n_exps"), u)
                        pe.wait_ge(s("c_turned_kept"), u)
                        next(both, None)
                        pe.wait_ge(s("d_combined"), u)
                        pe.wait_ge(s("n_turned_kept"), u)
                        d_output(r, t)
                        d_values(r, t, u)
                    n_tail(par, 3, hh * 4 + 4)
                    pe.wait_ge(s("v_masked"), hh + 2)
                    for m in range(4):
                        last = mm(banks[:, 6, bass.ds(448 + 8 * m + hh, 1)], v_masked[:, m // 2, P * (m % 2):P * (m % 2) + P],
                                  ones[:, 0:1], start=True, stop=True)
                    last.then_inc(s("v_picked"), 1)

            def n_tail(par, t, u):
                pe.wait_ge(s("n_probs"), u)
                pe.wait_ge(s("d_read"), u + 1)
                pe.wait_ge(s("n_read"), u)
                n_output(t)
                n_values(par, t, u + 1)

            def selected_half(n):
                pe.wait_ge(s("sel_placed"), n + 1)
                for q in range(8):
                    last = mm(banks[32 * (q // 4):32 * (q // 4) + 32, 4, :], q_sel[:, 8 * n + q, :], sel_kv[:, q, :, 0:64],
                              start=q % 4 == 0, stop=q % 4 == 3, tile_position=(0, 32 * (q // 4)))
                last.then_inc(s("sel_scored"), 1)
                pe.wait_ge(s("sel_row_max"), n + 1)
                tr(banks[0:1, 5, 0:64], small[0:64, 0:1], ident[0:64, 0:64]).then_inc(s("sel_max_turned"), 1)
                pe.wait_ge(s("sel_max_paired"), n + 1)
                mm(banks[0:64, 5, 64:65], sel_line[0:1, 0:64], ones[0:1, 0:1], start=True, stop=True).then_inc(s("sel_max_back"), 1)
                pe.wait_ge(s("sel_exps"), n + 1)
                mm(banks[0:64, 5, 72:73], const("pair")[0:64, 0:64], small[0:64, 2:3], start=True, stop=True).then_inc(s("sel_summed"), 1)
                pe.wait_ge(s("sel_probs"), n + 1)
                for m in range(SP_SLOTS):
                    last = tr(banks[0:64, 4, 64 * m:64 * m + 64], p_sel[:, 64 * m:64 * m + 64], ident[0:64, 0:64])
                last.then_inc(s("sel_probs_turned"), 1)
                pe.wait_ge(s("sel_probs_kept"), n + 1)
                pe.wait_ge(s("sel_new_in"), 64 * (n + 1))
                for q in range(8):
                    for m in range(SP_SLOTS):
                        last = mm(banks[64 * (q % 2):64 * (q % 2) + 64, 5, 128 + 4 * (q // 2):132 + 4 * (q // 2)],
                                  sel_kv[:, q, m, 64:128], p_sel_t[:, m, 4 * q:4 * q + 4], start=m == 0, stop=m == SP_SLOTS - 1,
                                  tile_position=(0, 64 * (q % 2)))
                last.then_inc(s("sel_out"), 1)

            pe.wait_ge(s("work_ready"), 1)
            for h2 in range(2):
                with pe.Fori(0, 2) as i:
                    attend_heads(h2, i)
                selected_half(h2)

            pe.wait_ge(s("sel_out_kept"), 2)
            for br in range(3):
                for r in range(GRP):
                    last = tr(banks[0:DEC, br, P * r:P * r + P], o_parts[:, br, :, r], ident)
            pe.wait_ge(s("o_diff_kept"), 1)
            for m in range(4):
                last = tr(banks[0:DEC, 3, P * m:P * m + P], o_diff[:, m, :], ident)
            last.then_inc(s("new_out_turned"), 1)
            pe.wait_ge(s("w_out_in"), 16)
            for t in range(TILES + 1):
                rows = P if t < TILES else DEC
                o = proj[:, t, 0:1024] if t < TILES else sample[:, 0:1024]
                u = t % 2
                pe.wait_ge(s("gated"), t + 1)
                if t == 0:
                    pe.wait_ge(s("new_out_read"), 1)
                if t >= 1:
                    pe.wait_ge(s("o_t_kept"), t)
                for k in range(KC):
                    last = tr(banks[:, k // 4, rows * (k % 4):rows * (k % 4) + rows], o[:, P * k:P * k + P], ident[0:rows, 0:rows])
                last.then_inc(s("o_turned"), 1)
                pe.wait_ge(s("o_t_kept"), t + 1)
                if t >= 2:
                    pe.wait_ge(s("y_ready"), t - 1)
                for c in range(2):
                    for k in range(KC):
                        last = mm(banks[0:rows, 2 + 2 * u + c, :], o_t[:, u, k, 0:rows], w_out[:, k, 512 * c:512 * c + 512],
                                  start=k == 0, stop=k == KC - 1)
                last.then_inc(s("y_summed"), 1)

        @block.scalar
        def _(act):
            A = nc.scalar.activation

            act.wait_ge(s("setup_in"), 16 * N_SETUP)
            act.wait_ge(s("stats_cleared"), 1)
            for t in range(TILES):
                A(x_tok[:, t, :], x_tok[:, t, :], ACT.Square, accum_out=x_rs[:, t:t + 1])
            A(x_new, x_new, ACT.Square, accum_out=x_rs[0:DEC, TILES:TILES + 1]).then_inc(s("x_squared"), 1)

            def sigmoids(u):
                for kv in range(2):
                    last = A(sig[:, u, kv, 0:NCMP], banks[:, u, 256 * kv:256 * kv + NCMP], ACT.Exp,
                             bias=bias[:, 1, kv:kv + 1], scale=-1.0)
                last.then_inc(s("exps_ready"), 1)

            def keep_rows(b, u):
                A(kc_n[:, b, :] if isinstance(b, int) else kc_n[:, bass.ds(b, 1), :].rearrange("p o n -> p (o n)"),
                  banks[:, 4 + u, 0:256], ACT.Copy)
                A(vc_n[:, b, :] if isinstance(b, int) else vc_n[:, bass.ds(b, 1), :].rearrange("p o n -> p (o n)"),
                  banks[:, 4 + u, 256:512], ACT.Copy).then_inc(s("rows_kept"), 1)

            act.wait_ge(s("bias_kept"), 1)
            act.wait_ge(s("pre_ready"), 1)
            sigmoids(0)
            act.wait_ge(s("x_means"), 1)
            A(x_rs[:, :], x_rs[:, :], ACT.Sqrt).then_inc(s("x_roots"), 1)
            act.wait_ge(s("pre_ready"), 2)
            sigmoids(1)
            act.wait_ge(s("rows_ready"), 1)
            keep_rows(0, 0)
            with act.Fori(0, 3) as i:
                for u in range(2):
                    act.wait_ge(s("pre_ready"), 2 * i + u + 3)
                    act.wait_ge(s("hid_ready"), 2 * i + u + 1)
                    sigmoids(u)
                    act.wait_ge(s("rows_ready"), 2 * i + u + 2)
                    keep_rows(2 * i + u + 1, 1 - u)
            act.wait_ge(s("rows_ready"), 8)
            keep_rows(7, 1)

            act.wait_ge(s("new_means"), 1)
            A(stats[0:DEC, TILES, :], stats[0:DEC, TILES, :], ACT.Sqrt).then_inc(s("new_roots"), 1)
            act.wait_ge(s("kc_means"), 1)
            A(kc_stats[:, 0:32], kc_stats[:, 0:32], ACT.Sqrt).then_inc(s("kc_roots"), 1)
            for h in range(4):
                act.wait_ge(s("kc_turned"), h + 1)
                A(kc_t[:, 2 * h:2 * h + 2, :].rearrange("p b n -> p (b n)"), banks[:, h, :], ACT.Copy).then_inc(s("kc_t_ready"), 1)
            act.wait_ge(s("cmp_max"), 1)
            A(p_cmp[:, 0:NCMP], banks[0:64, 7, 0:NCMP], ACT.Exp, bias=small[0:64, 62:63],
              accum_out=small[0:64, 63:64]).then_inc(s("cmp_exps"), 1)
            act.wait_ge(s("lam_dots"), 1)
            A(small[:, 56:58], small[:, 56:58], ACT.Exp).then_inc(s("lam_exps"), 1)

            with act.Fori(0, 8) as c:
                for t in range(TILES):
                    act.wait_ge(s("proj_ready"), 4 * c + t + 1)
                    A(proj[:, t, bass.ds(c * CHUNK, CHUNK)], banks[:, 2 + t, :], ACT.Copy,
                      scale=x_rs[:, t:t + 1]).then_inc(s("proj_kept"), 1)

            act.wait_ge(s("diff_max"), 1)
            A(scores, scores, ACT.Exp, bias=work[:, 144:145], accum_out=work[:, 145:146]).then_inc(s("diff_exps"), 1)
            for h in range(4):
                act.wait_ge(s("probs_turned"), h + 1)
                A(probs_t[:, 8 * h:8 * h + 8, :].rearrange("p g n -> p (g n)"), banks[:, h, :], ACT.Copy).then_inc(s("probs_kept"), 1)
            act.wait_ge(s("p_means"), 1)
            A(stats[:, 0:TILES, :], stats[:, 0:TILES, :], ACT.Sqrt).then_inc(s("p_roots"), 1)
            for n in range(14):
                act.wait_ge(s("turned"), n + 1)
                to = q_t[:, n, :] if n < 8 else k_t[:, n - 8, :]
                A(to, banks[:, n % 4, :], ACT.Copy).then_inc(s("turned_kept"), 1)
            for kv in range(2):
                act.wait_ge(s("turned"), 15 + kv)
                for g in range(2):
                    for l2 in range(2):
                        to = p_rows[64 * l2:64 * l2 + 64, :, 16 * kv + 8 * g:16 * kv + 8 * g + 8]
                        of = banks[64 * g:64 * g + 64, (14 + kv) % 4, :].rearrange("p (u l t) -> p t u l", l=LP, t=2)[:, l2, :, :]
                        last = A(to, of, ACT.Copy)
                last.then_inc(s("turned_kept"), 1)
            act.wait_ge(s("p_compressed"), 1)
            act.wait_ge(s("p_stored"), 16 * 7)
            for kv in range(2):
                last = A(p_sig[:, kv, 0:P_NCMP], banks[:, 4, 32 * kv:32 * kv + P_NCMP], ACT.Exp,
                         bias=bias[:, 1, kv:kv + 1], scale=-1.0)
            last.then_inc(s("p_exps"), 1)
            act.wait_ge(s("win_max"), 1)
            A(p_win, banks[0:64, 0, :], ACT.Exp, bias=work[0:64, 146:147], accum_out=work[0:64, 147:148]).then_inc(s("win_exps"), 1)
            act.wait_ge(s("p_kc_means"), 1)
            A(kc_stats[0:32, 32:34], kc_stats[0:32, 32:34], ACT.Sqrt).then_inc(s("p_kc_roots"), 1)
            A(gates, gates, ACT.Exp, scale=-1.0)
            A(new_gates, new_gates, ACT.Exp, scale=-1.0).then_inc(s("gate_exps"), 1)
            act.wait_ge(s("pads_cleared"), 1)

            def pad_queries(par, r):
                for c in range(2):
                    at = 64 * par + 32 * c
                    A(q_pad[at:at + 32, 3 * par + c, :], q_t[at:at + 32, bass.ds(r, 1), :].rearrange("p o n -> p (o n)"), ACT.Copy)
                A(q_pad[64 * par:64 * par + 64, 3 * par + 2, :],
                  q_t[64 * par:64 * par + 64, bass.ds(4 + r, 1), :].rearrange("p o n -> p (o n)"), ACT.Copy).then_inc(s("q_padded"), 1)

            for h2 in range(2):
                with act.Fori(0, 2) as i:
                    for par in range(2):
                        r = 2 * h2 + i
                        hh = 2 * r + par
                        if par == 0:
                            act.wait_ge(s("n_read"), 4 * hh + 1)
                            pad_queries(0, r)
                        for t in range(TILES):
                            u = 4 * hh + t + 1
                            n = P * (t + 1)
                            act.wait_ge(s("d_max"), u)
                            for c in range(2):
                                last = A(e_bufs[:, c, 0:n], banks[:, c, 0:n], ACT.Exp, bias=work[:, 148 + c:149 + c],
                                         accum_out=work[:, 150 + c:151 + c])
                            last.then_inc(s("d_exps"), 1)
                            if t == 0 and par == 0:
                                pad_queries(1, r)
                            if t > 0:
                                act.wait_ge(s("n_turned"), u - 1)
                                A(p_pct, banks[0:32, 2, 0:P], ACT.Copy).then_inc(s("c_turned_kept"), 1)
                            act.wait_ge(s("n_max"), u)
                            for c in range(2):
                                A(e_bufs[:, 2 + c, 0:n], banks[:, 2 + c, 0:n], ACT.Exp, bias=work[:, 152 + c:153 + c],
                                  accum_out=work[:, 156 + c:157 + c])
                            A(p_pc, p_pc, ACT.Exp, bias=work[:, 154:155]).then_inc(s("n_exps"), 1)
                            act.wait_ge(s("d_turned"), u)
                            A(d_pt[:, 0:n], banks[:, 4, 0:n], ACT.Copy).then_inc(s("d_turned_kept"), 1)
                        act.wait_ge(s("n_turned"), 4 * hh + 4)
                        A(p_pct, banks[0:32, 2, 0:P], ACT.Copy).then_inc(s("c_turned_kept"), 1)
                act.wait_ge(s("sel_max_neg"), h2 + 1)
                A(p_sel, banks[0:64, 4, :], ACT.Exp, bias=small[0:64, 1:2], accum_out=small[0:64, 2:3]).then_inc(s("sel_exps"), 1)

            act.wait_ge(s("new_out_read"), 1)
            for t in range(TILES + 1):
                z = proj[:, t, 3072:4096] if t < TILES else sample[:, 3072:4096]
                A(z_exp(t), z, ACT.Exp, scale=-1.0).then_inc(s("z_exps"), 1)
            act.wait_ge(s("out_means"), 1)
            A(out_stats[:, :, :], out_stats[:, :, :], ACT.Sqrt).then_inc(s("out_roots"), 1)
            for t in range(TILES + 1):
                rows = P if t < TILES else DEC
                u = t % 2
                act.wait_ge(s("o_turned"), t + 1)
                if t >= 2:
                    act.wait_ge(s("y_summed"), t - 1)
                for h in range(2):
                    last = A(o_t[:, u, 4 * h:4 * h + 4, 0:rows], banks[:, h, 0:4 * rows].rearrange("p (k n) -> p k n", k=4), ACT.Copy)
                last.then_inc(s("o_t_kept"), 1)

        @block.vector
        def _(dve):
            V = nc.vector
            chain = Chain(dve, "vector_steps")
            L = chain.link

            def tile_of(ap, t):
                return ap[:, t, :] if isinstance(t, int) else ap[:, bass.ds(t, 1), :].rearrange("p o n -> p (o n)")

            def rotate(x, table, half, heads, rows, t1, t2):
                cc = bc(table[0:rows, 0:2 * half], heads, 1)
                s1 = bc(table[0:rows, 2 * half:3 * half], heads, 1)
                s2 = bc(table[0:rows, 3 * half:4 * half], heads, 1)
                V.tensor_tensor(t1, x[:, :, 0:2 * half], cc, ALU.mult)
                V.tensor_tensor(t2[:, :, 0:half], x[:, :, half:2 * half], s1, ALU.mult)
                L(V.tensor_tensor(t2[:, :, half:2 * half], x[:, :, 0:half], s2, ALU.mult))
                return V.tensor_tensor(x[:, :, 0:2 * half], t1, t2, ALU.add)

            def head_means(x, st, tmp, rows):
                V.tensor_tensor(tmp[:, 0:1024], x[:, 0:1024], x[:, 0:1024], ALU.mult)
                L(V.tensor_tensor(tmp[:, 1024:1792], x[:, C_QN:C_VS], x[:, C_QN:C_VS], ALU.mult))
                V.tensor_reduce(st[:, 0:N_NORM32], tmp[:, 0:1024].rearrange("p (h d) -> p h d", d=DQ), AX.X, ALU.add)
                L(V.tensor_reduce(st[:, N_NORM32:N_STAT], tmp[:, 1024:1792].rearrange("p (h d) -> p h d", d=HD), AX.X, ALU.add))
                V.tensor_scalar(st[:, 0:N_NORM32], st[:, 0:N_NORM32], 1.0 / DQ, EPS, ALU.mult, ALU.add)
                return V.tensor_scalar(st[:, N_NORM32:N_STAT], st[:, N_NORM32:N_STAT], 1.0 / HD, EPS, ALU.mult, ALU.add)

            def head_scales(st):
                L(V.reciprocal(st, st))
                V.tensor_scalar(st[..., 0:16], st[..., 0:16], Q_SCALE_D, None, ALU.mult)
                L(V.tensor_scalar(st[..., 32:40], st[..., 32:40], Q_SCALE_N, None, ALU.mult))

            def head_norm(x, st, tmp, rows, table):
                x32 = x[:, 0:1024].rearrange("p (h d) -> p h d", d=DQ)
                x64 = x[:, C_QN:C_VS].rearrange("p (h d) -> p h d", d=HD)
                V.tensor_tensor(x32, x32, st[:, 0:32].unsqueeze(2).broadcast_to([rows, 32, DQ]), ALU.mult)
                L(V.tensor_tensor(x64, x64, st[:, 32:44].unsqueeze(2).broadcast_to([rows, 12, HD]), ALU.mult))
                for at, n, d, w in ((0, 16, DQ, 0), (16, 16, DQ, 32)):
                    y = x32[:, at:at + n, :]
                    V.tensor_tensor(y, y, bc(params[0:rows, w:w + d], n, 1), ALU.mult)
                for at, n, w in ((0, 8, 64), (8, 2, 128), (10, 2, 192)):
                    y = x64[:, at:at + n, :]
                    last = V.tensor_tensor(y, y, bc(params[0:rows, w:w + HD], n, 1), ALU.mult)
                L(last)
                rotate(x64, table[:, 0:32], 8, 12, rows, tmp[:, 0:192].rearrange("p (h n) -> p h n", h=12),
                       tmp[:, 192:384].rearrange("p (h n) -> p h n", h=12))
                return rotate(x32, table[:, 32:48], 4, 32, rows, tmp[:, 384:640].rearrange("p (h n) -> p h n", h=32),
                              tmp[:, 640:896].rearrange("p (h n) -> p h n", h=32))

            V.memset(x_rs[:, :], 1.0)
            V.memset(stats[:, :, :], 1.0)
            V.memset(kc_stats[:, :], 1.0).then_inc(s("stats_cleared"), 1)
            V.memset(ones[:, :], 1.0)
            V.memset(q_nsa[:, :, :], 0.0)
            V.memset(q_sel[:, :, :], 0.0)
            V.memset(hid[:, :, :, NCMP:256], 0.0)
            dve.sem_inc(s("rows_kept"), 1)
            dve.sem_inc(s("proj_kept"), 4)
            dve.sem_inc(s("scores_kept"), 2)
            for name in ("d_exps", "n_exps", "c_turned_kept", "n_turned_kept", "d_read", "n_read", "v_masked"):
                dve.sem_inc(s(name), 1)
            dve.wait_ge(s("setup_in"), 16 * N_SETUP)
            for k in range(KC):
                last = V.tensor_scalar(xt[:, k, :], xt[:, k, :], norm_w[:, k:k + 1], None, ALU.mult)
            last.then_inc(s("x_scaled"), 1)
            dve.wait_ge(s("bias_ready"), 1)
            V.tensor_copy(bias[:, 0, :], banks[:, 6, 0:2])
            V.tensor_scalar(bias[:, 1, :], banks[:, 6, 0:2], -1.0, None, ALU.mult).then_inc(s("bias_kept"), 1)
            dve.wait_ge(s("bias_kept"), 1)

            def hidden(pre, sg, h, kvs, n):
                L(V.tensor_scalar(sg, sg, 1.0, None, ALU.add))
                L(V.reciprocal(sg, sg))
                for kv in range(2):
                    last = V.scalar_tensor_tensor(h[:, kv, 0:n], pre[kv], bias[:, 0, kv:kv + 1], sg[:, kv, :], ALU.add, ALU.mult)
                return last

            def a_hidden(u):
                pre = [banks[:, u, 256 * kv:256 * kv + NCMP] for kv in range(2)]
                hidden(pre, sig[:, u, :, 0:NCMP], hid[:, u, :, :], 2, NCMP).then_inc(s("hid_ready"), 1)

            def sum_new(b, u):
                to = sample[:, b * CHUNK:(b + 1) * CHUNK] if isinstance(b, int) else sample[:, bass.ds(b * CHUNK, CHUNK)]
                L(V.tensor_copy(to, banks[0:DEC, 2 + u, :]))
                L(V.tensor_tensor(to, to, banks[32:32 + DEC, 2 + u, :], ALU.add))
                L(V.tensor_tensor(to, to, banks[64:64 + DEC, 2 + u, :], ALU.add))
                V.tensor_tensor(to, to, banks[96:96 + DEC, 2 + u, :], ALU.add).then_inc(s("new_proj_used"), 1)

            dve.wait_ge(s("exps_ready"), 1)
            a_hidden(0)
            dve.wait_ge(s("new_proj_ready"), 1)
            sum_new(0, 0)
            dve.wait_ge(s("x_squared"), 1)
            V.tensor_scalar(x_rs[:, :], x_rs[:, :], 1.0 / D_MODEL, EPS, ALU.mult, ALU.add).then_inc(s("x_means"), 1)
            dve.wait_ge(s("exps_ready"), 2)
            a_hidden(1)
            dve.wait_ge(s("new_proj_ready"), 2)
            sum_new(1, 1)
            dve.wait_ge(s("x_roots"), 1)
            L(V.reciprocal(x_rs[:, :], x_rs[:, :]))
            with dve.Fori(0, 3) as i:
                chain.loop(i, 10)
                for u in range(2):
                    dve.wait_ge(s("exps_ready"), 2 * i + u + 3)
                    dve.wait_ge(s("rows_ready"), 2 * i + u + 1)
                    a_hidden(u)
                    dve.wait_ge(s("new_proj_ready"), 2 * i + u + 3)
                    sum_new(2 * i + u + 2, u)
                chain.end(3, 10)
            dve.wait_ge(s("new_proj_used"), 8)

            tmp = proj[:, 0, :]
            tmp_k = proj[:, 1, 0:2048].rearrange("p (h d) -> p h d", d=HD)
            dve.wait_ge(s("pre_ready"), 8)
            L(V.tensor_scalar(sample[:, :], sample[:, :], x_rs[0:DEC, TILES:TILES + 1], None, ALU.mult))
            new_st = stats[0:DEC, TILES, :]
            head_means(sample[:, :], new_st, tmp[0:DEC, :], DEC).then_inc(s("new_means"), 1)
            dve.wait_ge(s("rows_kept"), 9)
            kc_v = kc_n.rearrange("p b (h d) -> p (b h) d", d=HD)
            L(V.tensor_tensor(tmp_k, kc_v, kc_v, ALU.mult))
            L(V.tensor_reduce(kc_stats[:, 0:32], tmp_k, AX.X, ALU.add))
            V.tensor_scalar(kc_stats[:, 0:32], kc_stats[:, 0:32], 1.0 / HD, EPS, ALU.mult, ALU.add).then_inc(s("kc_means"), 1)
            dve.wait_ge(s("new_roots"), 1)
            head_scales(new_st)
            head_norm(sample[:, :], new_st, tmp[0:DEC, :], DEC, rope[:, TILES, :]).then_inc(s("new_normed"), 1)
            dve.wait_ge(s("kc_roots"), 1)
            L(V.reciprocal(kc_stats[:, 0:32], kc_stats[:, 0:32]))
            L(V.tensor_tensor(kc_v, kc_v, kc_stats[:, 0:32].unsqueeze(2).broadcast_to([P, 32, HD]), ALU.mult))
            L(V.tensor_tensor(kc_v, kc_v, bc(params[:, 256:320], 32, 1), ALU.mult))
            t1 = proj[:, 1, 0:256].rearrange("p (h n) -> p h n", h=16)
            t2 = proj[:, 1, 256:512].rearrange("p (h n) -> p h n", h=16)
            kc_tiles = kc_n.rearrange("p b (n h d) -> p n b h d", n=2, d=HD)
            for nt in range(2):
                for g in range(2):
                    x = kc_tiles[:, nt, :, g, :]
                    last = rotate(x, ropec[:, nt, :], 8, DEC, P, t1[:, 0:DEC, :], t2[:, 0:DEC, :])
                    if nt + g < 2:
                        L(last)
            last.then_inc(s("kc_normed"), 1)
            dve.wait_ge(s("new_turned"), 1)
            turned = banks[:, 6, 0:112].rearrange("p (n b) -> p n b", b=DEC)
            L(V.memset(q_blk, 0.0))
            for cc in range(4):
                rows = slice(32 * cc, 32 * cc + 32)
                to = bass.AP(tensor=small8, offset=32 * cc * 2048 + cc, ap=[[2048, 32], [256, 4], [36, 8]])
                V.tensor_copy(to, turned[rows, 0:4, :])
            for g in range(2):
                to = bass.AP(tensor=q_nsa, offset=64 * g * 512 + 4 * g, ap=[[512, 64], [72, 8], [1, 4]])
                V.tensor_copy(to, turned[64 * g:64 * g + 64, 4:8, :].rearrange("p r b -> p b r"))
                for par in range(2):
                    for b0 in range(2):
                        to = bass.AP(tensor=q_sel, offset=64 * par * 512 + 80 * b0 + 40 * g + 4 * par, ap=[[512, 64], [128, 4], [1, 4]])
                        V.tensor_copy(to, turned[64 * g:64 * g + 64, 4:8, :].rearrange("p r (b c) -> p c b r", c=2)[:, b0, :, :])
            V.tensor_copy(k_new[:, :, :], turned[:, 8:14, :]).then_inc(s("q_placed"), 1)

            dve.wait_ge(s("cmp_scored"), 1)
            V.tensor_reduce(small[0:64, 62:63], banks[0:64, 7, 0:NCMP], AX.X, ALU.max, negate=True).then_inc(s("cmp_max"), 1)
            dve.wait_ge(s("own_scored"), 1)
            V.tensor_copy(scores[:, PAST:PAST + 1], banks[:, 5, 0:1]).then_inc(s("own_kept"), 1)
            L(V.memset(p_cmp[:, NCMP:256], 0.0))
            dve.wait_ge(s("cmp_exps"), 1)
            L(V.reciprocal(small[0:64, 63:64], small[0:64, 63:64]))
            V.tensor_scalar(p_cmp, p_cmp, small[0:64, 63:64], None, ALU.mult).then_inc(s("cmp_probs"), 1)
            dve.wait_ge(s("cmp_probs_turned"), 1)
            L(V.tensor_copy(p_cmp_t, banks[:, 6, 256:384].rearrange("p (n m) -> p n m", n=2)))
            V.tensor_reduce(group_p.rearrange("p n m -> p (n m)"), p_cmp_t.rearrange("p n (m r) -> p (n m) r", r=GRP),
                            AX.X, ALU.add).then_inc(s("group_probs"), 1)
            dve.wait_ge(s("importance"), 1)
            L(V.tensor_copy(imp, banks[0:16, 4, 0:2 * N_CAND]))
            dve.wait_ge(s("cmp_out"), 1)
            for g in range(2):
                rows = slice(64 * g, 64 * g + 64)
                last = V.tensor_copy(o_parts[rows, 0, :, :], banks[rows, 3, 128:192].rearrange("p (b h r) -> p b h r", h=2, r=GRP)[:, :, g, :])
            last.then_inc(s("cmp_out_kept"), 1)
            pairs = xn[0:16, 0:N_CAND * N_CAND].rearrange("p (j i) -> p j i", i=N_CAND)
            others = bc(imp[:, N_CAND:2 * N_CAND], N_CAND, 1)
            mine = imp[:, 0:N_CAND].unsqueeze(2).broadcast_to([16, N_CAND, N_CAND])
            at = CONST_COLS["later"][0]
            later = bass.AP(tensor=consts, offset=at, ap=[[consts.shape[1], 16], [1, N_CAND], [1, N_CAND]])
            L(V.tensor_tensor(pairs, others, mine, ALU.is_gt))
            L(V.tensor_reduce(rank, pairs, AX.X, ALU.add))
            L(V.tensor_tensor(pairs, others, mine, ALU.is_equal))
            L(V.tensor_tensor(pairs, pairs, later, ALU.mult))
            L(V.tensor_reduce(rank2, pairs, AX.X, ALU.add))
            L(V.tensor_tensor(rank, rank, rank2, ALU.add))
            dve.wait_ge(s("pages_bg_in"), 16)
            L(V.tensor_copy(block_row, pages_bg[:, :].unsqueeze(2).broadcast_to([16, PAGES, 2])))
            L(V.scalar_tensor_tensor(block_row_flat, block_row_flat, 4.0, const("blockrow")[0:16, :], ALU.mult, ALU.add))
            chosen = xn[0:16, 0:N_TOP * N_CAND].rearrange("p (s j) -> p s j", j=N_CAND)
            L(V.tensor_tensor(chosen, bc(rank, N_TOP, 1), const("slots")[0:16, :].unsqueeze(2).broadcast_to([16, N_TOP, N_CAND]),
                              ALU.is_equal))
            L(V.tensor_tensor(chosen, chosen, bc(block_row_flat[:, 1:1 + N_CAND], N_TOP, 1), ALU.mult))
            V.tensor_reduce(slot_row[:, 2:15], chosen, AX.X, ALU.add).then_inc(s("ranked"), 1)
            V.tensor_copy(slot_row[:, 0:1], block_row_flat[:, 0:1])
            V.tensor_copy(slot_row[:, 1:2], block_row_flat[:, 63:64])
            L(V.tensor_copy(slot_row[:, 15:16], block_row_flat[:, 0:1]))
            for par in range(2):
                one = slot_row.rearrange("p (m t) -> p t m", t=2)[:, par, :]
                last = V.tensor_tensor(spread[0:16, P * par:P * par + P].rearrange("p (q m) -> p q m", m=SP_SLOTS),
                                       bc(one, 16, 1), const("eye16")[0:16, :].unsqueeze(2).broadcast_to([16, 16, SP_SLOTS]), ALU.mult)
            last.then_inc(s("rows_spread"), 1)
            lam = params[:, 384:512].rearrange("p (a b d) -> p a b d", a=2, b=2)
            L(V.tensor_tensor(lam_work.rearrange("p (a d) -> p a d", a=2), lam[:, :, 0, :], lam[:, :, 1, :], ALU.mult))
            V.tensor_reduce(small[:, 56:58], lam_work.rearrange("p (a d) -> p a d", a=2), AX.X, ALU.add).then_inc(s("lam_dots"), 1)

            with dve.Fori(0, 4) as i:
                for u in range(2):
                    dve.wait_ge(s("k_used"), 16 * i + 8 * u + 8)
                    V.tensor_copy(wide[:, bass.ds(i * 1024 + u * 512, 512)], banks[:, u, :]).then_inc(s("scores_kept"), 1)
            dve.wait_ge(s("scores_kept"), 10)

            V.tensor_reduce(work[:, 144:145], scores, AX.X, ALU.max, negate=True).then_inc(s("diff_max"), 1)
            dve.wait_ge(s("index_spread"), 1)
            L(V.tensor_scalar(spread[:, 0:P], banks[:, 6, 0:P], 64.0, None, ALU.mult))
            V.tensor_scalar(index[:, :], spread[:, 0:P], const("iota64"), None, ALU.add).then_inc(s("index_ready"), 1)
            dve.wait_ge(s("lam_exps"), 1)
            L(V.tensor_tensor(work[:, 158:159], small[:, 57:58], small[:, 56:57], ALU.subtract))
            L(V.tensor_scalar(work[:, 158:159], work[:, 158:159], -LAM_INIT, None, ALU.add))
            L(V.tensor_tensor(small[:, 58:59], const("e12")[:, 1:2], work[:, 158:159], ALU.mult))
            L(V.tensor_tensor(small[:, 58:59], small[:, 58:59], const("e12")[:, 0:1], ALU.add))
            dve.wait_ge(s("diff_exps"), 1)
            L(V.reciprocal(work[:, 145:146], work[:, 145:146]))
            L(V.tensor_tensor(small[:, 58:59], small[:, 58:59], work[:, 145:146], ALU.mult))
            V.tensor_scalar(own_rows, const("bmap"), scores[:, PAST:PAST + 1], None, ALU.mult)
            V.tensor_scalar(own_weights, const("hmap"), small[:, 58:59], None, ALU.mult)
            V.tensor_scalar(d_weights, const("dmap"), small[:, 58:59], None, ALU.mult).then_inc(s("diff_weights"), 1)
            dve.wait_ge(s("proj_kept"), 36)
            with dve.Fori(0, TILES) as t:
                chain.loop(t, 3)
                L(head_means(tile_of(proj, t), tile_of(stats, t), xt_flat[:, 0:1792], P))
                chain.end(TILES, 3)
            dve.sem_inc(s("p_means"), 1)
            dve.wait_ge(s("own_weighted"), 1)
            V.tensor_copy(own_a, banks[0:DEC, 4, 0:DH]).then_inc(s("own_read"), 1)
            dve.wait_ge(s("p_roots"), 1)
            head_scales(stats[:, 0:TILES, :])
            with dve.Fori(0, TILES) as t:
                chain.loop(t, 5)
                L(head_norm(tile_of(proj, t), tile_of(stats, t), xt_flat[:, 0:896], P, tile_of(rope, t)))
                chain.end(TILES, 5)
            dve.sem_inc(s("norm_done"), 1)
            dve.wait_ge(s("win_in"), 16)
            V.tensor_copy(win_kt[:, :, 0], k_new[:, 5, :]).then_inc(s("win_key_placed"), 1)
            dve.wait_ge(s("p_exps"), 1)
            dve.wait_ge(s("p_stored"), 16 * 7)
            V.memset(p_hid[:, :, P_NCMP:32], 0.0)
            pre = [banks[:, 4, 32 * kv:32 * kv + P_NCMP] for kv in range(2)]
            hidden(pre, p_sig[:, :, 0:P_NCMP], p_hid, 2, P_NCMP).then_inc(s("p_hid"), 1)
            dve.wait_ge(s("win_scored"), 1)
            V.tensor_reduce(work[0:64, 146:147], banks[0:64, 0, :], AX.X, ALU.max, negate=True).then_inc(s("win_max"), 1)
            dve.wait_ge(s("p_rows_ready"), 1)
            V.tensor_copy(p_vc, banks[0:32, 5, P:2 * P])
            L(V.tensor_copy(p_kc, banks[0:32, 5, 0:P]))
            kc2 = p_kc.rearrange("p (h d) -> p h d", d=HD)
            p_tmp = proj[0:32, 2, 1536:1664].rearrange("p (h d) -> p h d", d=HD)
            L(V.tensor_tensor(p_tmp, kc2, kc2, ALU.mult))
            L(V.tensor_reduce(kc_stats[0:32, 32:34], p_tmp, AX.X, ALU.add))
            V.tensor_scalar(kc_stats[0:32, 32:34], kc_stats[0:32, 32:34], 1.0 / HD, EPS, ALU.mult, ALU.add).then_inc(s("p_kc_means"), 1)
            dve.wait_ge(s("win_exps"), 1)
            L(V.reciprocal(work[0:64, 147:148], work[0:64, 147:148]))
            V.tensor_scalar(p_win, p_win, work[0:64, 147:148], None, ALU.mult).then_inc(s("win_probs"), 1)
            dve.wait_ge(s("p_kc_roots"), 1)
            L(V.reciprocal(kc_stats[0:32, 32:34], kc_stats[0:32, 32:34]))
            L(V.tensor_tensor(kc2, kc2, kc_stats[0:32, 32:34].unsqueeze(2).broadcast_to([32, 2, HD]), ALU.mult))
            L(V.tensor_tensor(kc2, kc2, bc(params[0:32, 256:320], 2, 1), ALU.mult))
            rotate(kc2, ropec[:, 0, :], 8, 2, 32, proj[0:32, 2, 1536:1568].rearrange("p (h n) -> p h n", h=2),
                   proj[0:32, 2, 1568:1600].rearrange("p (h n) -> p h n", h=2)).then_inc(s("p_kc_normed"), 1)
            dve.wait_ge(s("p_kc_turned"), 1)
            L(V.tensor_copy(p_kc_t, banks[:, 5, 256:288]))
            dve.wait_ge(s("win_probs_turned"), 1)
            V.tensor_copy(p_win_t, banks[:, 1, 0:256].rearrange("p (k m) -> p k m", k=4)).then_inc(s("win_probs_kept"), 1)
            dve.wait_ge(s("win_out"), 1)
            for g in range(2):
                rows = slice(64 * g, 64 * g + 64)
                V.tensor_copy(o_parts[rows, 2, :, :], banks[rows, 1, 256:320].rearrange("p (b h r) -> p b h r", h=2, r=GRP)[:, :, g, :])
            dve.wait_ge(s("gate_exps"), 1)
            for g_ap in (gates, new_gates):
                L(V.tensor_scalar(g_ap, g_ap, 1.0, None, ALU.add))
                L(V.reciprocal(g_ap, g_ap))
            V.memset(q_pad, 0.0).then_inc(s("pads_cleared"), 1)
            dve.sem_inc(s("work_ready"), 1)

            def d_first(u, t):
                n = P * (t + 1)
                dve.wait_ge(s("d_scored"), u)
                diag = banks[:, 0:2, P * t:P * t + P]
                L(V.tensor_tensor(diag, diag, bc(const("causal"), 2, 1), ALU.add))
                V.tensor_reduce(work[:, 148:150], banks[:, 0:2, 0:n], AX.X, ALU.max, negate=True).then_inc(s("d_max"), 1)

            def d_combine(u, t):
                n = P * (t + 1)
                dve.wait_ge(s("d_exps"), u + 1)
                L(V.reciprocal(work[:, 150:152], work[:, 150:152]))
                V.tensor_scalar(e_bufs[:, 0, 0:n], e_bufs[:, 0, 0:n], work[:, 150:151], None, ALU.mult)
                L(V.tensor_tensor(work[:, 151:152], work[:, 151:152], work[:, 158:159], ALU.mult))
                V.scalar_tensor_tensor(e_bufs[:, 0, 0:n], e_bufs[:, 1, 0:n], work[:, 151:152], e_bufs[:, 0, 0:n],
                                       ALU.mult, ALU.add).then_inc(s("d_combined"), 1)

            def n_first(u, t):
                n = P * (t + 1)
                dve.wait_ge(s("n_scored"), u)
                diag = banks[:, 2:4, P * t:P * t + P]
                V.tensor_tensor(diag, diag, bc(const("causal"), 2, 1), ALU.add)
                L(V.tensor_tensor(p_pc, banks[:, 6, 480:512], const("cmpneg")[:, 32 * t:32 * t + 32], ALU.add))
                V.tensor_reduce(work[:, 154:155], p_pc, AX.X, ALU.max, negate=True)
                V.tensor_reduce(work[:, 152:154], banks[:, 2:4, 0:n], AX.X, ALU.max, negate=True).then_inc(s("n_max"), 1)

            def n_second(u, t, hh):
                dve.wait_ge(s("n_exps"), u + 1)
                L(V.tensor_tensor(p_pc, p_pc, const("cmp01")[:, 32 * t:32 * t + 32], ALU.mult))
                L(V.tensor_reduce(work[:, 155:156], p_pc, AX.X, ALU.add))
                L(V.tensor_scalar(work[:, 155:156], work[:, 155:156], 1e-30, None, ALU.max))
                L(V.reciprocal(work[:, 155:158], work[:, 155:158]))
                V.tensor_tensor(small[:, 48:51], work[:, 155:158],
                                gates_by_head[:, t, :, bass.ds(hh, 1)].rearrange("p b o -> p (b o)"), ALU.mult).then_inc(s("n_probs"), 1)

            def n_move(u, t):
                n = P * (t + 1)
                dve.wait_ge(s("n_turned"), u)
                V.tensor_copy(n_pt[:, :, 0:n], banks[:, 4:6, 0:n]).then_inc(s("n_turned_kept"), 1)

            def n_last(u, t, hh, par):
                dve.wait_ge(s("n_out"), u)
                o = proj[:, t, bass.ds(64 * hh, 64)]
                at = 64 * par
                dve.wait_ge(s("n_probs"), u)
                L(V.tensor_scalar(o, banks[:, 5, at:at + 64], small[:, 49:50], None, ALU.mult))
                L(V.scalar_tensor_tensor(o, banks[:, 5, P + at:P + at + 64], small[:, 50:51], o, ALU.mult, ALU.add))
                V.scalar_tensor_tensor(o, banks[:, 5, 256:320], small[:, 48:49], o, ALU.mult, ALU.add).then_inc(s("n_read"), 1)

            def d_last(u, t, hh, par):
                dve.wait_ge(s("d_out"), u)
                V.tensor_copy(proj[:, t, bass.ds(512 + 64 * hh, 64)], banks[:, 4, 64 * par:64 * par + 64]).then_inc(s("d_read"), 1)

            def selected_half(n):
                dve.wait_ge(s("sel_in"), 16 * 64 * (n + 1))
                for g in range(2):
                    to = sel_kv[64:128, :, SP_SLOTS - 1, 0].rearrange("p (b h) -> p h b", h=2)[:, g, :]
                    last = V.tensor_copy(to, k_new[64 * g:64 * g + 64, 4, 4 * n:4 * n + 4])
                last.then_inc(s("sel_placed"), 1)
                dve.wait_ge(s("sel_scored"), n + 1)
                new = banks[0:64, 4, 448:512]
                L(V.tensor_tensor(new, new, const("selmask")[0:64, :], ALU.add))
                V.tensor_reduce(small[0:64, 0:1], banks[0:64, 4, :], AX.X, ALU.max).then_inc(s("sel_row_max"), 1)
                dve.wait_ge(s("sel_max_turned"), n + 1)
                halves = banks[0:1, 5, 0:64].rearrange("p (q t r) -> p q t r", t=2, r=GRP)
                line = sel_line.rearrange("p (q t r) -> p q t r", t=2, r=GRP)
                L(V.tensor_copy(line, halves))
                L(V.tensor_tensor(line[:, :, 0, :], line[:, :, 0, :], halves[:, :, 1, :], ALU.max))
                V.tensor_copy(line[:, :, 1, :], line[:, :, 0, :]).then_inc(s("sel_max_paired"), 1)
                dve.wait_ge(s("sel_max_back"), n + 1)
                V.tensor_scalar(small[0:64, 1:2], banks[0:64, 5, 64:65], -1.0, None, ALU.mult).then_inc(s("sel_max_neg"), 1)
                dve.wait_ge(s("sel_summed"), n + 1)
                L(V.reciprocal(small[0:64, 3:4], banks[0:64, 5, 72:73]))
                V.tensor_scalar(p_sel, p_sel, small[0:64, 3:4], None, ALU.mult).then_inc(s("sel_probs"), 1)
                dve.wait_ge(s("sel_probs_turned"), n + 1)
                for par in range(2):
                    of = banks[0:64, 4, :].rearrange("p (m q t r) -> p t m q r", m=SP_SLOTS, t=2, r=GRP)[:, par, :, :, :]
                    last = V.tensor_copy(p_sel_t[64 * par:64 * par + 64, :, :].rearrange("p m (q r) -> p m q r", r=GRP), of)
                last.then_inc(s("sel_probs_kept"), 1)
                dve.wait_ge(s("sel_out"), n + 1)
                V.tensor_copy(o_parts[:, 1, 4 * n:4 * n + 4, :], banks[:, 5, 128:144].rearrange("p (b r) -> p b r", r=GRP)
                              ).then_inc(s("sel_out_kept"), 1)

            C_LINKS = 80
            for h2 in range(2):
                with dve.Fori(0, 2) as i:
                    chain.loop(i, C_LINKS)
                    for par in range(2):
                        r = 2 * h2 + i
                        hh = 2 * r + par
                        for t in range(TILES):
                            u = 4 * hh + t + 1
                            d_first(u, t)
                            if t > 0:
                                n_second(u - 1, t - 1, hh)
                                n_move(u - 1, t - 1)
                            if t == 0:
                                n_first(u, t)
                            d_combine(u, t)
                            if t > 0:
                                n_last(u - 1, t - 1, hh, par)
                                n_first(u, t)
                            d_last(u, t, hh, par)
                        n_second(4 * hh + 4, 3, hh)
                        n_move(4 * hh + 4, 3)
                        n_last(4 * hh + 4, 3, hh, par)
                        dve.wait_ge(s("v_used"), 8 * hh + 8)
                        own = const("diag").rearrange("p (b h) -> p b h", b=4)
                        for m in range(2):
                            last = V.tensor_tensor(v_masked[:, m, :].rearrange("p (h v) -> p h v", v=DV),
                                                   banks[:, 7, 256 * m:256 * m + 256].rearrange("p (h v) -> p h v", v=DV),
                                                   own[:, bass.ds(2 * i + par, 1), 4 * m:4 * m + 4].rearrange("p o h -> p (o h)")
                                                   .unsqueeze(2).broadcast_to([P, 4, DV]), ALU.mult)
                        last.then_inc(s("v_masked"), 1)
                    chain.end(2, C_LINKS)
                selected_half(h2)
            dve.wait_ge(s("n_read"), 33)
            dve.wait_ge(s("d_read"), 33)
            dve.sem_inc(s("attended"), 1)
            dve.wait_ge(s("v_picked"), 8)
            V.tensor_copy(o_diff[:, :, :], banks[:, 6, 448:480].rearrange("p (m b) -> p m b", b=DEC)).then_inc(s("o_diff_kept"), 1)

            dve.wait_ge(s("new_out_turned"), 1)
            o_new = sample[:, 0:512].rearrange("p (h d) -> p h d", d=HD)
            d_new = sample[:, 512:1024].rearrange("p (h d) -> p h d", d=HD)
            scratch = wide[0:DEC, 2048:2560].rearrange("p (h d) -> p h d", d=HD)
            dve.wait_ge(s("s_stored"), 16 * 7)
            for br in range(3):
                w = new_gates.rearrange("p (b h) -> p b h", b=3)[:, br, :].unsqueeze(2).broadcast_to([DEC, NH, HD])
                of = banks[0:DEC, br, :].rearrange("p (h d) -> p h d", d=HD)
                L(V.tensor_tensor(scratch if br else o_new, of, w, ALU.mult))
                if br:
                    L(V.tensor_tensor(o_new, o_new, scratch, ALU.add))
            L(V.tensor_tensor(scratch, sample[:, C_VD:C_VD + 512].rearrange("p (h d) -> p h d", d=HD),
                              own_a.unsqueeze(2).broadcast_to([DEC, DH, DV]), ALU.mult))
            V.tensor_tensor(d_new, scratch, banks[0:DEC, 3, :].rearrange("p (h d) -> p h d", d=HD), ALU.add).then_inc(s("new_out_read"), 1)
            dve.wait_ge(s("new_out_read"), 1)
            for t in range(TILES + 1):
                rows = P if t < TILES else DEC
                o = (proj[:, t, 512:1024] if t < TILES else sample[:, 512:1024]).rearrange("p (h d) -> p h d", d=DV)
                sq = wide[0:rows, 2048:2560].rearrange("p (h d) -> p h d", d=DV)
                L(V.tensor_tensor(sq, o, o, ALU.mult))
                L(V.tensor_reduce(out_stats[0:rows, t, :], sq, AX.X, ALU.add))
            V.tensor_scalar(out_stats, out_stats, 1.0 / DV, EPS, ALU.mult, ALU.add).then_inc(s("out_means"), 1)
            dve.wait_ge(s("out_roots"), 1)
            L(V.reciprocal(out_stats, out_stats))
            L(V.tensor_scalar(out_stats, out_stats, 1.0 - LAM_INIT, None, ALU.mult))
            for t in range(TILES + 1):
                rows = P if t < TILES else DEC
                whole = proj[:, t, :] if t < TILES else sample[:, :]
                o = whole[:, 512:1024].rearrange("p (h d) -> p h d", d=DV)
                z, e = whole[:, 3072:4096], z_exp(t)
                L(V.tensor_tensor(o, o, out_stats[0:rows, t, :].unsqueeze(2).broadcast_to([rows, DH, DV]), ALU.mult))
                L(V.tensor_tensor(o, o, bc(params[0:rows, 320:384], DH, 1), ALU.mult))
                dve.wait_ge(s("z_exps"), t + 1)
                L(V.tensor_scalar(e, e, 1.0, None, ALU.add))
                L(V.reciprocal(e, e))
                L(V.tensor_tensor(e, e, z, ALU.mult))
                V.tensor_tensor(whole[:, 0:1024], whole[:, 0:1024], e, ALU.mult).then_inc(s("gated"), 1)
            for t in range(TILES + 1):
                rows = P if t < TILES else DEC
                u = t % 2
                dve.wait_ge(s("y_summed"), t + 1)
                dve.wait_ge(s("x_in"), 32)
                y = proj[:, t, 1024:2048] if t < TILES else sample[:, 0:1024]
                x = x_again[:, t, :] if t < TILES else x_new_again
                V.tensor_tensor(y.rearrange("p (c n) -> p c n", c=2), banks[0:rows, 2 + 2 * u:4 + 2 * u, :],
                                x.rearrange("p (c n) -> p c n", c=2), ALU.add).then_inc(s("y_ready"), 1)

        @block.gpsimd
        def _(pool):
            pool.dma_start(pages_bg[:, :], src["pages_bg"][:, :]).then_inc(s("pages_bg_in"), 16)
            pool.wait_ge(s("index_ready"), 1)
            pool.wait_ge(s("proj_ready"), 32)
            for n in range(2):
                if n:
                    pool.wait_ge(s("sel_out"), 1)
                for q in range(8):
                    for m in range(SP_SLOTS):
                        col = (8 * n + q) * SP_SLOTS + m
                        nc.gpsimd.indirect_dma_start(
                            out=sel_kv[:, q, m, :], out_offset=None, in_=src["sel_cache"][:, :],
                            in_offset=bass.IndirectOffsetOnAxis(ap=index[:, col:col + 1], axis=0)).then_inc(s("sel_in"), 16)
                pool.wait_ge(s("sel_in"), 16 * 64 * (n + 1))
                for b in range(4):
                    pool.dma_start(sel_kv[64:65, 2 * b:2 * b + 2, SP_SLOTS - 1, 64:128],
                                   sample[4 * n + b:4 * n + b + 1, C_VS:C_VS + P].rearrange("p (g v) -> p g v", g=2)
                                   ).then_inc(s("sel_new_in"), 16)
    return nc


_OUTS = {"y_p": (SEQ, D_MODEL), "y_s": (DEC, D_MODEL), "p_cmp": (SEQ, 256), "p_sel": (SEQ, 256), "p_win": (SEQ, 256),
         "p_dk": (SEQ, 512), "p_dv": (SEQ, 512), "s_cmp": (DEC, 256), "s_sel": (DEC, 256), "s_win": (DEC, SEQ, 256),
         "s_dk": (DEC, 512), "s_dv": (DEC, 512)}


def build(nc, arrays):
    src = {k: nc.dram_tensor(f"in_{k}", a.shape, mybir.dt.from_np(a.dtype), kind="ExternalInput").ap() for k, a in arrays.items()}
    dst = {k: nc.dram_tensor(f"out_{k}", shape, F32, kind="ExternalOutput").ap() for k, shape in _OUTS.items()}
    program(nc, src, dst)


def kernel(**inputs):
    import concourse.bacc as _bacc
    from concourse.bass_utils import run_bass_kernel_spmd as _run

    arrays = laid_out({k: np.asarray(v) for k, v in inputs.items()})
    nc = _bacc.Bacc("TRN2", target_bir_lowering=False, num_devices=1, dynamic_dma_scratch_size=4096)
    build(nc, arrays)
    r = _run(nc, [{f"in_{k}": a for k, a in arrays.items()}], core_ids=[0]).results[0]
    got = {k: np.asarray(r[f"out_{k}"]) for k in _OUTS}
    p_kv, s_kv = (1, 1, SEQ, 2, NKV, HD), (1, DEC, 1, 2, NKV, HD)
    return (got["y_p"].reshape(1, SEQ, D_MODEL), got["y_s"].reshape(DEC, 1, D_MODEL),
            got["p_cmp"].reshape(p_kv), got["p_sel"].reshape(p_kv), got["p_win"].reshape(p_kv),
            got["p_dk"].reshape(1, 1, SEQ, DH, 2, DQ), got["p_dv"].reshape(1, 1, SEQ, DH, DV),
            got["s_cmp"].reshape(s_kv), got["s_sel"].reshape(s_kv), got["s_win"].reshape(1, DEC, SEQ, 2, NKV, HD),
            got["s_dk"].reshape(1, DEC, 1, DH, 2, DQ), got["s_dv"].reshape(1, DEC, 1, DH, DV))
```
